# Optimizing a Trainium2 kernel written in Bass

```python
import jax, jax.numpy as jnp
from jax import lax
import numpy as np

D_MODEL = 1024
BATCH = 1
SEQ = 2048
DEPTH = 1
DEC_BATCH = 1
DEC_SEQ = 64
PAST_LEN = 1024

CHUNK = 64
D_MIX = D_MODEL
D_CONV = D_MIX // 2
CONV_GROUPS = 8
CONV_W = 3
D_GLA = D_MIX - D_CONV
N_HEADS = 4
HEAD_V = D_GLA // N_HEADS
HEAD_K = HEAD_V // 2
D_QK = N_HEADS * HEAD_K
GATE_RANK = 16
GATE_TAU = 16.0
D_FF = 2816
FFN_CONV_W = 3
EPS = 1e-6
D_IN_PROJ = 3 * D_CONV + 2 * D_QK + D_GLA + GATE_RANK + D_GLA
SPLITS = list(np.cumsum([D_CONV, D_CONV, D_CONV, D_QK, D_QK, D_GLA, GATE_RANK])[:].tolist())

kernel_name = "hybrid_conv_gla_streaming_encoder_step"

def rmsnorm(x, g):
    xf = x.astype(jnp.float32)
    y = xf * lax.rsqrt(jnp.mean(xf * xf, axis=-1, keepdims=True) + EPS) * g.astype(jnp.float32)
    return y.astype(x.dtype)

def causal_dwconv(u, prev, w):
    width = w.shape[0]
    L = u.shape[1]
    up = jnp.concatenate([prev.astype(u.dtype), u], axis=1)
    y = up[:, 0:L] * w[0]
    for t in range(1, width):
        y = y + up[:, t:t + L] * w[t]
    return y, up[:, L:]

def gla(q, k, v, logg, s0):
    Bsz, L, H, _ = q.shape
    V = v.shape[-1]
    C = min(CHUNK, L)
    N = L // C
    f32 = jnp.float32

    def blk(t):
        return t.astype(f32).reshape(Bsz, N, C, H, t.shape[-1]).transpose(1, 0, 3, 2, 4)

    q, k, v, logg = blk(q), blk(k), blk(v), blk(logg)
    b = jnp.cumsum(logg, axis=3)
    b_last = b[:, :, :, -1:, :]
    qt = q * jnp.exp(b)
    kt = k * jnp.exp(-b)
    kd = k * jnp.exp(b_last - b)
    mask = jnp.tril(jnp.ones((C, C), dtype=bool))
    att = jnp.where(mask, jnp.einsum('nbhik,nbhjk->nbhij', qt, kt), 0.0)
    o_intra = jnp.einsum('nbhij,nbhjv->nbhiv', att, v)
    ds = jnp.einsum('nbhck,nbhcv->nbhkv', kd, v)
    decay = jnp.exp(b_last[:, :, :, 0, :])

    def step(s, inp):
        d, dsn = inp
        return d[..., None] * s + dsn, s

    s_final, s_start = lax.scan(step, s0.astype(f32), (decay, ds))
    o = o_intra + jnp.einsum('nbhik,nbhkv->nbhiv', qt, s_start)
    o = o.transpose(1, 0, 3, 2, 4).reshape(Bsz, L, H, V)
    return o, s_final.astype(s0.dtype)

def mixer(xn, conv_prev, gla_prev, w_in, w_alpha, b_alpha, conv_w, g_conv, g_gla, w_out):
    Bsz, L, _ = xn.shape
    z = xn @ w_in
    bg, cg, h, q, k, v, gr, r = jnp.split(z, SPLITS, axis=-1)
    cv, conv_new = causal_dwconv(cg * h, conv_prev, conv_w)
    y_conv = rmsnorm(bg * cv, g_conv)
    logg = jax.nn.log_sigmoid((gr @ w_alpha + b_alpha).astype(jnp.float32)) / GATE_TAU
    q = q.reshape(Bsz, L, N_HEADS, HEAD_K) * (HEAD_K ** -0.5)
    k = k.reshape(Bsz, L, N_HEADS, HEAD_K)
    v = v.reshape(Bsz, L, N_HEADS, HEAD_V)
    logg = logg.reshape(Bsz, L, N_HEADS, HEAD_K)
    o, gla_new = gla(q, k, v, logg, gla_prev)
    o = rmsnorm(o, g_gla).astype(xn.dtype).reshape(Bsz, L, D_GLA)
    y_gla = o * jax.nn.silu(r)
    y = jnp.concatenate([y_conv, y_gla], axis=-1) @ w_out
    return y, conv_new, gla_new

def conv_ffn(xn, prev, w_up, conv_w, w_down):
    u = xn @ w_up
    uc, new = causal_dwconv(u, prev, conv_w)
    a, g = jnp.split(uc, 2, axis=-1)
    return (jax.nn.silu(g) * a) @ w_down, new

def trunk(x, conv_s, gla_s, ffn_s, w_in, w_alpha, b_alpha, conv_w, g_conv, g_gla, w_out,
          norm1, norm2, w_up, ffn_conv_w, w_down, final_norm):
    new_c, new_g, new_f = [], [], []
    for l in range(DEPTH):
        y, c, g = mixer(rmsnorm(x, norm1[l]), conv_s[l], gla_s[l], w_in[l], w_alpha[l], b_alpha[l],
                        conv_w[l], g_conv[l], g_gla[l], w_out[l])
        x = x + y
        y, f = conv_ffn(rmsnorm(x, norm2[l]), ffn_s[l], w_up[l], ffn_conv_w[l], w_down[l])
        x = x + y
        new_c.append(c)
        new_g.append(g)
        new_f.append(f)
    return rmsnorm(x, final_norm), jnp.stack(new_c), jnp.stack(new_g), jnp.stack(new_f)

def setup_inputs(seed: int = 0) -> dict:
    key = jax.random.key(seed)
    ks = jax.random.split(key, 20)
    f32 = jnp.float32
    nrm = lambda k, s, sc: jax.random.normal(k, s, f32) * sc
    return {
        "x_prompt": nrm(ks[0], (BATCH, SEQ, D_MODEL), 1.0),
        "x_sample": nrm(ks[1], (DEC_BATCH, DEC_SEQ, D_MODEL), 1.0),
        "state_conv": nrm(ks[2], (DEPTH, DEC_BATCH, CONV_W - 1, D_CONV), 1.0),
        "state_gla": nrm(ks[3], (DEPTH, DEC_BATCH, N_HEADS, HEAD_K, HEAD_V), 1.0),
        "state_ffn_conv": nrm(ks[4], (DEPTH, DEC_BATCH, FFN_CONV_W - 1, 2 * D_FF), 1.0),
        "w_in": nrm(ks[5], (DEPTH, D_MODEL, D_IN_PROJ), D_MODEL ** -0.5),
        "w_alpha": nrm(ks[6], (DEPTH, GATE_RANK, D_QK), GATE_RANK ** -0.5),
        "b_alpha": nrm(ks[7], (DEPTH, D_QK), 0.01),
        "conv_w": nrm(ks[8], (DEPTH, CONV_W, D_CONV), CONV_W ** -0.5),
        "g_conv": 1.0 + nrm(ks[9], (DEPTH, D_CONV), 0.02),
        "g_gla": 1.0 + nrm(ks[10], (DEPTH, HEAD_V), 0.02),
        "w_out": nrm(ks[11], (DEPTH, D_MIX, D_MODEL), D_MIX ** -0.5),
        "norm1": 1.0 + nrm(ks[12], (DEPTH, D_MODEL), 0.02),
        "norm2": 1.0 + nrm(ks[13], (DEPTH, D_MODEL), 0.02),
        "w_up": nrm(ks[14], (DEPTH, D_MODEL, 2 * D_FF), D_MODEL ** -0.5),
        "ffn_conv_w": nrm(ks[15], (DEPTH, FFN_CONV_W, 2 * D_FF), FFN_CONV_W ** -0.5),
        "w_down": nrm(ks[16], (DEPTH, D_FF, D_MODEL), D_FF ** -0.5),
        "final_norm": 1.0 + nrm(ks[17], (D_MODEL,), 0.02),
    }

def reference(x_prompt, x_sample, state_conv, state_gla, state_ffn_conv, w_in, w_alpha, b_alpha,
              conv_w, g_conv, g_gla, w_out, norm1, norm2, w_up, ffn_conv_w, w_down, final_norm):
    weights = (w_in, w_alpha, b_alpha, conv_w, g_conv, g_gla, w_out,
               norm1, norm2, w_up, ffn_conv_w, w_down, final_norm)
    bp = x_prompt.shape[0]
    dt = x_prompt.dtype
    zc = jnp.zeros((DEPTH, bp, CONV_W - 1, D_CONV), dt)
    zg = jnp.zeros((DEPTH, bp, N_HEADS, HEAD_K, HEAD_V), dt)
    zf = jnp.zeros((DEPTH, bp, FFN_CONV_W - 1, 2 * D_FF), dt)
    y_prompt, pc, pg, pf = trunk(x_prompt, zc, zg, zf, *weights)
    y_sample, sc, sg, sf = trunk(x_sample, state_conv, state_gla, state_ffn_conv, *weights)
    return (y_prompt, y_sample, pc, pg, pf, sc, sg, sf)


_drawn_inputs = setup_inputs


def setup_inputs(seed=0):
    import zlib

    import numpy as np

    out = dict(_drawn_inputs(seed))
    spreads = {}
    factors = {'b_alpha': 8.0, 'g_conv': 4.526, 'g_gla': 6.947, 'norm2': 2.73, 'final_norm': 2.863}
    for name, (base, spread) in spreads.items():
        noise = np.random.default_rng([zlib.crc32(name.encode()), seed]).standard_normal(out[name].shape)
        drawn = base * np.exp(spread * noise) if base else spread * noise
        out[name] = __import__('jax').numpy.asarray(drawn.astype(out[name].dtype))
    for name, factor in factors.items():
        out[name] = (out[name] * factor).astype(out[name].dtype)
    return out
```

```python
from contextlib import ExitStack

import concourse.bass as bass
from concourse import mybir

F32 = mybir.dt.float32
F32R = mybir.dt.float32r
U32 = mybir.dt.uint32
ACT = mybir.ActivationFunctionType
ALU = mybir.AluOpType

P = 128
D = 1024
KT = D // P
SEQ = 2048
DEC = 64
D_CONV = 512
CJ = D_CONV // P
HEADS = 4
HK = 64
HV = 128
RANK = 16
TAU = 16.0
D_FF = 2816
NF = D_FF // P
EPS = 1e-6
CHUNK = 64
C_BG, C_CG, C_H = 0, D_CONV, 2 * D_CONV
C_Q = 3 * D_CONV
C_K = C_Q + HEADS * HK
C_V = C_K + HEADS * HK
C_GR = C_V + HEADS * HV
C_R = C_GR + RANK

BT = SEQ // 2
GAP = 2
NCOL = [BT, BT + GAP + DEC]
TILES = [BT // P, BT // P + 1]
CHUNKS = [[(0, 512), (512, 512)], [(0, 364), (364, 364), (728, 362)]]
WMAX = NCOL[1]
SLOTS = 4

BEFORE = {
    "r": (0, 0, 0, 0), "qk": (0, 0, 0, 0), "gr": (2, 0, 0, 0), "v": (3, 2, 2, 2),
    "conv": (4, 3, 3, 3), "out": (8, 7, 7, 3), "ffn": (10, 9, 9, 5), "end": (32, 31, 20, 16),
}
FFN_TAP, FFN_PREV, CONV_TAP, CONV_PREV, G_CONV, G_GLA = 0, 3, 5, 8, 10, 11
B_GATE, B_ATT, B_O, B_DS = 3, 4, 5, 6


def tile_cols(t):
    return (t * P, P) if t < BT // P else (BT + GAP, DEC)


def tile_row(b, t):
    return (b * BT + t * P, False) if t < BT // P else (0, True)


def chunk_of_end(b, t):
    end = sum(tile_cols(t)) - 1
    return next(c for c, (c0, n) in enumerate(CHUNKS[b]) if end < c0 + n)


def last_tile_of(b, c):
    c0, n = CHUNKS[b][c]
    return max(t for t in range(TILES[b]) if tile_cols(t)[0] < c0 + n)


def unit_index(b, stage, slot, i):
    return b * BEFORE["end"][slot] + BEFORE[stage][slot] + i


def wait(eng, sem, value):
    if isinstance(value, int) and value <= 0:
        return
    eng.wait_ge(sem, value)


def build(nc, x_prompt, x_sample, state_conv, state_gla, state_ffn, w_in, w_alpha, b_alpha, conv_w,
          g_conv, g_gla, w_out, norm1, norm2, w_up, ffn_conv_w, w_down, final_norm,
          y_prompt, y_sample, conv_prompt, gla_prompt, ffn_prompt, conv_sample, gla_sample, ffn_sample):
    with ExitStack() as ctx:
        def sem(name):
            return ctx.enter_context(nc.semaphore(name))

        def place(name, at, shape, dt=F32):
            size = 4
            for n in shape[1:]:
                size *= n
            return nc.alloc_sbuf_tensor_at(name, shape, dt, offset=at), -(-(at + size) // 32) * 32

        at = -(-nc.sbuf_base // 32) * 32
        xt_hi, at = place("xt_hi", at, [P, KT, WMAX], F32R)
        xt_lo, at = place("xt_lo", at, [P, KT, WMAX], F32R)
        w_hi, at = place("w_hi", at, [P, SLOTS, D], F32R)
        w_lo, at = place("w_lo", at, [P, SLOTS, D], F32R)
        raw, at = place("raw", at, [P, SLOTS, D])
        gain, at = place("gain", at, [P, D])
        ident, at = place("ident", at, [P, P])
        tri, at = place("tri", at, [P, P])
        ones, at = place("ones", at, [P, P])
        params, at = place("params", at, [P, 12, 2 * NF])
        zeros4, at = place("zeros4", at, [P, 2, 2])
        ffn_half, at = place("ffn_half", at, [P, 2, 2 * NF])
        ffn_tail, at = place("ffn_tail", at, [P, 2, 2 * NF])
        ffn_tail_s, at = place("ffn_tail_s", at, [P, 2, 2 * NF])
        conv_tail, at = place("conv_tail", at, [P, 2, CJ])
        conv_tail_s, at = place("conv_tail_s", at, [P, 2, CJ])
        gla_s, at = place("gla_s", at, [P, 2, HV])
        gla_s_smp, at = place("gla_s_smp", at, [P, 2, HV])
        w_al, at = place("w_al", at, [RANK, 2 * P])
        b_al, at = place("b_al", at, [P, 2 * P])
        eps_t, at = place("eps_t", at, [P, 1])
        ssq, at = place("ssq", at, [P, 2])
        msq, at = place("msq", at, [P, 2])
        rstd, at = place("rstd", at, [P, 2])
        decay, at = place("decay", at, [P, 2, 2])
        resid_at = at
        resid, at = place("resid", resid_at, [P, TILES[1], D])
        qk, then = place("qk", resid_at, [P, 4, WMAX])
        v_tok, then = place("v_tok", then, [P, TILES[1], HEADS * HV])
        assert then <= at
        arena_at = at
        gla_y, at = place("gla_y", arena_at, [P, HEADS, WMAX])
        conv_y, at = place("conv_y", at, [P, CJ, WMAX])
        conv_u, at = place("conv_u", at, [P, 2 + WMAX])
        rs_conv, _ = place("rs_conv", at - 4384, [P, WMAX])
        free_at = at
        gate_in, at = place("gate_in", free_at, [RANK, WMAX])
        lg, at = place("lg", at, [P, 2 * P])
        soft, at = place("soft", at, [P, 2 * P])
        b_cum, at = place("b_cum", at, [P, 2, P])
        q_exp, at = place("q_exp", at, [P, 2, 2, P])
        k_exp, at = place("k_exp", at, [P, 2, P])
        k_end, at = place("k_end", at, [P, 2, P])
        k_end_t, at = place("k_end_t", at, [P, 2, 2 * P])
        att, at = place("att", at, [P, HEADS, P])
        o_sq, at = place("o_sq", at, [P, HEADS, P])
        assert at <= nc.sbuf_usable_end, (at, nc.sbuf_usable_end)
        x_in, at = place("x_in", free_at, [P, 2, D])
        x_n, at = place("x_n", at, [P, 2, D])
        conv_sq, _ = place("conv_sq", at - 8192, [P, CJ, 512])
        assert at <= nc.sbuf_usable_end
        hid_hi, at = place("hid_hi", arena_at, [P, 2, WMAX], F32R)
        hid_lo, at = place("hid_lo", at, [P, 2, WMAX], F32R)
        up_u, at = place("up_u", at, [P, 2, 2 + WMAX])
        up_a, at = place("up_a", at, [P, WMAX])
        up_g, at = place("up_g", at, [P, 2, 512])
        assert at <= free_at
        rows, _ = place("rows", arena_at, [2 * NF, 12, P])
        tails_out, _ = place("tails_out", free_at, [2 * NF, 8, P])

        ps = ctx.enter_context(nc.psum_tensor("ps", [P, 8, 512], F32))

        raw_ready = [sem(f"raw_ready{s}") for s in range(SLOTS)]
        hi_ready = [sem(f"hi_ready{s}") for s in range(SLOTS)]
        lo_ready = [sem(f"lo_ready{s}") for s in range(SLOTS)]
        rows_zero, rows_ready, consts_ready, small_ready = sem("rows_zero"), sem("rows_ready"), sem("consts_ready"), sem("small_ready")
        rows_turned, params_ready = sem("rows_turned"), sem("params_ready")
        gain_ready = sem("gain_ready")
        smp_ready = sem("smp_ready")
        stored = [sem("stored0"), sem("stored1")]
        states_stored = sem("states_stored")
        tails_turned, tails_ready = sem("tails_turned"), sem("tails_ready")

        norm_sems = {name: sem(f"norm_{name}") for name in
                     ("loaded0", "loaded1", "squared", "mean", "rstd", "scaled", "turned", "hi", "lo")}

        class Norm:

            def __init__(self, b, kind):
                self.loaded = [norm_sems["loaded0"], norm_sems["loaded1"]]
                self.squared = norm_sems["squared"]
                self.mean = norm_sems["mean"]
                self.rstd = norm_sems["rstd"]
                self.scaled = norm_sems["scaled"]
                self.turned = norm_sems["turned"]
                self.hi = norm_sems["hi"]
                self.lo = norm_sems["lo"]
                done = 3 * TILES[0] * b + kind * TILES[b]
                turned = 2 * TILES[0] * b + kind * TILES[b]
                self.base = {"squared": done, "mean": done, "rstd": done, "scaled": done,
                             "turned": 2 * turned, "hi": 2 * turned, "lo": 2 * turned,
                             "loaded0": 16 * b * ((TILES[0] + 1) // 2), "loaded1": 16 * b * (TILES[0] // 2)}

            def wait(self, eng, name, value):
                if value > 0:
                    eng.wait_ge(norm_sems[name], self.base[name] + value)

        class Mix:

            def __init__(self, b):
                self.z_done = sem(f"z_done_{b}")
                self.z_read = sem(f"z_read_{b}")
                self.zeros = sem(f"zeros_{b}")
                self.c_done = sem(f"c_done_{b}")
                self.cg_read = sem(f"cg_read_{b}")
                self.u_done = sem(f"u_done_{b}")
                self.conv_step = sem(f"conv_step_{b}")
                self.y_done = sem(f"y_done_{b}")
                self.pre = sem(f"pre_{b}")
                self.pre_b = sem(f"pre_b_{b}")
                self.soft = sem(f"soft_{b}")
                self.lg = sem(f"lg_{b}")
                self.cum = sem(f"cum_{b}")
                self.cum_read = sem(f"cum_read_{b}")
                self.dist = sem(f"dist_{b}")
                self.k_end_exp = sem(f"k_end_exp_{b}")
                self.qk_exp = sem(f"qk_exp_{b}")
                self.att_done = sem(f"att_done_{b}")
                self.att_read = sem(f"att_read_{b}")
                self.turned = sem(f"turned_{b}")
                self.turned_read = sem(f"turned_read_{b}")
                self.d1 = sem(f"d1_{b}")
                self.d2 = sem(f"d2_{b}")
                self.state0 = sem(f"state0_{b}")
                self.state1 = sem(f"state1_{b}")
                self.o_squared = sem(f"o_squared_{b}")
                self.o_mean = sem(f"o_mean_{b}")
                self.o_rs = sem(f"o_rs_{b}")
                self.gla_step = sem(f"gla_step_{b}")
                self.gla_y = sem(f"gla_y_{b}")
                self.y_hi = sem(f"y_hi_{b}")
                self.y_lo = sem(f"y_lo_{b}")
                self.csq = sem(f"csq_{b}")
                self.cmean = sem(f"cmean_{b}")
                self.crs_step = sem(f"crs_step_{b}")
                self.crs = sem(f"crs_{b}")
                self.cy = sem(f"cy_{b}")
                self.out_done = sem(f"out_done_{b}")
                self.out_read = sem(f"out_read_{b}")
                self.gap = sem(f"gap_{b}")
                self.x_in = [sem(f"x_again0_{b}"), sem(f"x_again1_{b}")]

        class Ffn:

            def __init__(self, b):
                self.up_done = sem(f"up_done_{b}")
                self.up_read = sem(f"up_read_{b}")
                self.tap1 = sem(f"tap1_{b}")
                self.conv_done = sem(f"conv_done_{b}")
                self.silu = sem(f"silu_{b}")
                self.h_done = sem(f"h_done_{b}")
                self.h_hi = sem(f"h_hi_{b}")
                self.h_lo = sem(f"h_lo_{b}")
                self.down_done = sem(f"down_done_{b}")
                self.bank_free = sem(f"bank_free_{b}")

        first = [Norm(b, 0) for b in range(2)]
        second = [Norm(b, 1) for b in range(2)]
        final = [Norm(b, 2) for b in range(2)]
        mixes = [Mix(b) for b in range(2)]
        ffns = [Ffn(b) for b in range(2)]

        w_in_v = w_in[0].rearrange("(k p) c -> p k c", p=P)
        w_up_v = w_up[0].rearrange("(k p) c -> p k c", p=P)

        def x_rows(b, t):
            r, smp = tile_row(b, t)
            return (x_sample if smp else x_prompt)[0, r:r + tile_cols(t)[1], :]

        def y_rows(b, t):
            r, smp = tile_row(b, t)
            return (y_sample if smp else y_prompt)[0, r:r + tile_cols(t)[1], :]

        def in_unit(c0):
            return w_in_v[:, :, c0:c0 + P]

        Z_UNITS = [(C_R + P * u, u % 2, "r", u // 2) for u in range(HEADS)]
        Z_UNITS += [(C_Q + P * u, 2 + u % 2, "qk", u // 2) for u in range(4)]
        Z_UNITS += [(C_GR, 0, "gr", 0)]
        V_UNITS = [(C_V + P * h, h, "v", 0) for h in (1, 2, 3, 0)]

        def units(b):
            def one(u):
                c, s, stage, i = u
                return in_unit(c), s, unit_index(b, stage, s, i)

            def conv(j, m):
                return in_unit((C_CG, C_H, C_BG)[m] + P * j), m, unit_index(b, "conv", m, j)

            def out(n):
                k = (n + HEADS) % KT
                return w_out[0, k * P:(k + 1) * P, :], n % SLOTS, unit_index(b, "out", n % SLOTS, n // SLOTS)

            e = {}
            e["norm1", 1] = [one(Z_UNITS[0]), one(Z_UNITS[1])] if b == 0 else []
            e["norm1", 3] = [one(Z_UNITS[4]), one(Z_UNITS[5])]
            follow = {0: Z_UNITS[2], 1: Z_UNITS[3], 2: Z_UNITS[8], 3: V_UNITS[0], 4: Z_UNITS[6], 5: Z_UNITS[7],
                      6: V_UNITS[1], 7: V_UNITS[2], 8: V_UNITS[3]}
            for n, u in follow.items():
                e["z", n] = [one(u)]
            e["v", 0] = [conv(0, 0), conv(0, 1), conv(0, 2), out(3)]
            for j in range(CJ):
                for m in range(3):
                    e["conv", j, m] = [conv(j + 1, m)] if j + 1 < CJ else [out(m)]
            for p in range(2):
                e["out", p] = [out(4 + 2 * p), out(5 + 2 * p)]
            e["out", 2] = [up_unit(b, 0, 0), up_unit(b, 1, 0)]
            e["last", 0] = [one2(b + 1, 0)] if b == 0 else []
            e["last", 1] = [one2(b + 1, 1)] if b == 0 else []
            return e

        def one2(b, n):
            c, s, stage, i = Z_UNITS[n]
            return in_unit(c), s, unit_index(b, stage, s, i)

        def up_unit(b, m, f):
            return w_up_v[:, :, bass.ds(m * D_FF + f * P, P)], m, unit_index(b, "ffn", m, 0) + f

        def down_unit(b, f, par, pair):
            return w_down[0, bass.ds(f * P, P), :], 2 + par, unit_index(b, "ffn", 2 + par, 0) + pair

        def load_unit(sp, unit):
            src, s, n = unit
            wait(sp, lo_ready[s], n)
            dst = raw[:, s, :]
            if len(src.shape) == 3:
                dst = dst.rearrange("p (k c) -> p k c", k=KT)
            sp.dma_start(dst, src).then_inc(raw_ready[s], 16)

        def high_unit(act, unit, used=None):
            _, s, n = unit
            wait(act, raw_ready[s], 16 * (n + 1))
            if used:
                wait(act, *used)
            act.activation(w_hi[:, s, :], raw[:, s, :], ACT.Copy).then_inc(hi_ready[s], 1)

        def low_unit(pool, unit):
            _, s, n = unit
            wait(pool, hi_ready[s], n + 1)
            pool.tensor_tensor(w_lo[:, s, :], raw[:, s, :], w_hi[:, s, :].bitcast(F32),
                               ALU.subtract).then_inc(lo_ready[s], 1)

        def conv_events(b):
            groups = [(m, c) for m in range(3) for c in range(len(CHUNKS[b]))]
            steps = [("X", 0), ("Y", 0), ("Z", 0), ("X", 1), ("Y", 1), ("Z", 1)]
            out, g = [], 0
            for n, step in enumerate(steps):
                out.append(step)
                upto = (n + 1) * len(groups) // len(steps)
                while g < upto:
                    out.append(("G",) + groups[g])
                    g += 1
            return out

        def down_share(b, slot):
            nd, ns = 2 * TILES[b], 2 * len(CHUNKS[b])
            return range(slot * nd // ns, (slot + 1) * nd // ns)

        block = ctx.enter_context(nc.Block())

        @block.sync
        def _(sp):
            sp.wait_ge(rows_zero, 1)
            with nc.allow_non_contiguous_dma(reason="small parameters"):
                for i in range(3):
                    sp.dma_start(rows[:, FFN_TAP + i, :], ffn_conv_w[0, i].rearrange("(f p) -> f p", p=P)).then_inc(rows_ready, 16)
                    sp.dma_start(rows[0:CJ, CONV_TAP + i, :], conv_w[0, i].rearrange("(f p) -> f p", p=P)).then_inc(rows_ready, 16)
                for i in range(2):
                    sp.dma_start(rows[:, FFN_PREV + i, :], state_ffn[0, 0, i].rearrange("(f p) -> f p", p=P)).then_inc(rows_ready, 16)
                    sp.dma_start(rows[0:CJ, CONV_PREV + i, :], state_conv[0, 0, i].rearrange("(f p) -> f p", p=P)).then_inc(rows_ready, 16)
                sp.dma_start(rows[0:CJ, G_CONV, :], g_conv[0].rearrange("(f p) -> f p", p=P)).then_inc(rows_ready, 16)
                sp.dma_start(rows[0:1, G_GLA, :], g_gla).then_inc(rows_ready, 16)

            def load_gain(src):
                sp.dma_start(gain[:, :], src.partition_broadcast(P)).then_inc(gain_ready, 16)

            for b in range(2):
                mix, ffn, n1, n2, nf = mixes[b], ffns[b], first[b], second[b], final[b]
                prep = units(b)
                nt = TILES[b]

                def load_x(t, loaded):
                    m = tile_cols(t)[1]
                    sp.dma_start(x_in[0:m, t % 2, :], x_rows(b, t)).then_inc(loaded[t % 2], 16)

                if b == 1:
                    wait(sp, mixes[0].out_read, 8 * TILES[0])
                    final[0].wait(sp, "scaled", TILES[0])
                for t in range(nt):
                    n1.wait(sp, "scaled", t - 1)
                    load_x(t, n1.loaded)
                    if t == 1:
                        load_gain(norm1[0])
                        if b == 0:
                            sp.dma_start(w_al[:, :], w_alpha[0]).then_inc(small_ready, 16)
                            sp.dma_start(b_al[:, :], b_alpha[0].partition_broadcast(P)).then_inc(small_ready, 16)
                            sp.dma_start(gla_s_smp[:, :, :], state_gla[0, 0].rearrange("(q e) k v -> (e k) q v", e=2)).then_inc(small_ready, 16)
                    for u in prep.get(("norm1", t), []):
                        load_unit(sp, u)
                for n in range(9):
                    for u in prep["z", n]:
                        load_unit(sp, u)
                n1.wait(sp, "scaled", nt)
                load_gain(norm2[0])
                for u in prep["v", 0]:
                    load_unit(sp, u)
                for j in range(CJ):
                    for m in range(3):
                        for u in prep["conv", j, m]:
                            load_unit(sp, u)
                if b == 1:
                    sp.wait_ge(mix.state1, nt - 1)
                    sp.wait_ge(mix.state0, nt)
                    sp.dma_start(gla_prompt[0, 0].rearrange("(q e) k v -> (e k) q v", e=2), gla_s[:, :, :]).then_inc(states_stored, 16)
                    sp.dma_start(gla_sample[0, 0].rearrange("(q e) k v -> (e k) q v", e=2), gla_s_smp[:, :, :]).then_inc(states_stored, 16)
                sp.wait_ge(mix.gla_y, nt)
                load_x(0, mix.x_in)
                load_x(1, mix.x_in)
                for p in range(2):
                    for u in prep["out", p]:
                        load_unit(sp, u)
                for t in range(2, nt):
                    sp.wait_ge(mix.out_read, 2 * (t - 1))
                    load_x(t, mix.x_in)
                for u in prep["out", 2]:
                    load_unit(sp, u)
                load_unit(sp, down_unit(b, 0, 0, 0))
                load_unit(sp, up_unit(b, 0, 1))
                load_unit(sp, up_unit(b, 1, 1))
                n2.wait(sp, "scaled", nt)
                load_gain(final_norm)
                with sp.Fori(0, (NF - 2) // 2) as i:
                    for d in range(2):
                        f = i * 2 + (1 + d)
                        load_unit(sp, down_unit(b, f, (1 + d) % 2, i + (1 + d) // 2))
                        load_unit(sp, up_unit(b, 0, f + 1))
                        load_unit(sp, up_unit(b, 1, f + 1))
                load_unit(sp, down_unit(b, NF - 1, (NF - 1) % 2, (NF - 1) // 2))
                for m in range(2):
                    for u in prep["last", m]:
                        load_unit(sp, u)
                for t in range(nt):
                    nf.wait(sp, "scaled", t + 1)
                    m = tile_cols(t)[1]
                    sp.dma_start(y_rows(b, t), x_n[0:m, t % 2, :]).then_inc(stored[t % 2], 16)
            sp.wait_ge(tails_ready, 2)
            for i, dst in enumerate((ffn_prompt, ffn_sample)):
                for r in range(2):
                    sp.dma_start(dst[0, 0, r].rearrange("(f p) -> f p", p=P), tails_out[:, 2 * i + r, :]).then_inc(states_stored, 16)
            for i, dst in enumerate((conv_prompt, conv_sample)):
                for r in range(2):
                    sp.dma_start(dst[0, 0, r].rearrange("(f p) -> f p", p=P), tails_out[0:CJ, 4 + 2 * i + r, :]).then_inc(states_stored, 16)
            sp.wait_ge(states_stored, 16 * 10)
            for par in range(2):
                sp.wait_ge(stored[par], 16 * sum((nt + 1 - par) // 2 for nt in TILES))

        @block.gpsimd
        def _(pool):
            pool.memset(rows[:, :, :], 0.0).then_inc(rows_zero, 1)
            pool.memset(ident[:, :], 0.0).then_inc(consts_ready, 1)
            pool.memset(tri[:, :], 1.0).then_inc(consts_ready, 1)
            pool.memset(ones[:, :], 1.0).then_inc(consts_ready, 1)
            pool.memset(eps_t[:, :], EPS).then_inc(consts_ready, 1)
            pool.memset(zeros4[:, :, :], 0.0).then_inc(consts_ready, 1)
            pool.memset(conv_tail[:, :, :], 0.0).then_inc(consts_ready, 1)
            pool.memset(gla_s[:, :, :], 0.0).then_inc(consts_ready, 1)
            pool.memset(xt_hi[:, :, BT:BT + GAP].bitcast(F32), 0.0).then_inc(consts_ready, 1)
            pool.memset(xt_lo[:, :, BT:BT + GAP].bitcast(F32), 0.0).then_inc(consts_ready, 1)
            pool.wait_ge(consts_ready, 9)
            pool.affine_select(out=ident[:, :], in_=ident[:, :], compare_op=ALU.not_equal, fill=1.0, base=0,
                               pattern=[[-1, P]], channel_multiplier=1).then_inc(consts_ready, 1)
            pool.affine_select(out=tri[:, :], in_=tri[:, :], compare_op=ALU.is_ge, fill=0.0, base=0,
                               pattern=[[1, P]], channel_multiplier=-1).then_inc(consts_ready, 1)
            pool.wait_ge(consts_ready, 11)
            pool.memset(tri[0:CHUNK, CHUNK:P], 0.0).then_inc(consts_ready, 1)

            for b in range(2):
                mix, ffn, n1, n2, nf = mixes[b], ffns[b], first[b], second[b], final[b]
                prep = units(b)
                nt, nch = TILES[b], len(CHUNKS[b])
                for t in range(nt):
                    for u in prep.get(("norm1", t), []):
                        low_unit(pool, u)
                for n in range(9):
                    if n == 1:
                        n1.wait(pool, "turned", 2 * nt)
                        pool.memset(q_exp[:, :, :, :], 0.0).then_inc(mix.zeros, 1)
                        pool.memset(k_end_t[:, :, :], 0.0).then_inc(mix.zeros, 1)
                        pool.memset(att[:, :, :], 0.0).then_inc(mix.zeros, 1)
                    for u in prep["z", n]:
                        low_unit(pool, u)
                for u in prep["v", 0]:
                    low_unit(pool, u)
                for j in range(CJ):
                    for m in range(3):
                        for u in prep["conv", j, m]:
                            low_unit(pool, u)
                for n in range(HEADS):
                    pool.wait_ge(mix.y_hi, n + 1)
                    pool.tensor_tensor(xt_lo[:, HEADS + n, 0:NCOL[b]], gla_y[:, n, 0:NCOL[b]],
                                       xt_hi[:, HEADS + n, 0:NCOL[b]].bitcast(F32), ALU.subtract).then_inc(mix.y_lo, 1)
                for n in range(CJ):
                    pool.wait_ge(mix.y_hi, HEADS + n + 1)
                    pool.tensor_tensor(xt_lo[:, n, 0:NCOL[b]], conv_y[:, n, 0:NCOL[b]],
                                       xt_hi[:, n, 0:NCOL[b]].bitcast(F32), ALU.subtract).then_inc(mix.y_lo, 1)
                for p in range(3):
                    for u in prep["out", p]:
                        low_unit(pool, u)

                def ffn_step(f, par, pair, nxt):
                    low_unit(pool, down_unit(b, f, par, pair))
                    if nxt is not None:
                        low_unit(pool, nxt(0))
                    for c, (c0, n) in enumerate(CHUNKS[b]):
                        i = f * nch + c
                        g = up_g[:, (par * nch + c) % 2, 0:n]
                        pool.wait_ge(ffn.h_hi, i + 1)
                        pool.tensor_tensor(hid_lo[:, par, c0:c0 + n], g, hid_hi[:, par, c0:c0 + n].bitcast(F32),
                                           ALU.subtract).then_inc(ffn.h_lo, 1)
                    if nxt is not None:
                        low_unit(pool, nxt(1))

                ffn_step(0, 0, 0, lambda m: up_unit(b, m, 1))
                with pool.Fori(0, (NF - 2) // 2) as i:
                    for d in range(2):
                        f = i * 2 + (1 + d)
                        ffn_step(f, (1 + d) % 2, i + (1 + d) // 2, lambda m, f=f: up_unit(b, m, f + 1))
                ffn_step(NF - 1, (NF - 1) % 2, (NF - 1) // 2, (lambda m: prep["last", m][0]) if b == 0 else None)

        @block.scalar
        def _(act):
            def norm_rstd(norm, t, src):
                m = tile_cols(t)[1]
                i = slice(t % 2, t % 2 + 1)
                act.activation(x_n[0:m, t % 2, :], src, ACT.Square, accum_out=ssq[0:m, i]).then_inc(norm.squared, 1)
                norm.wait(act, "squared", t + 1)
                act.activation(msq[0:m, i], ssq[0:m, i], ACT.Ln, scale=1 / D, bias=eps_t[0:m, :]).then_inc(norm.mean, 1)
                norm.wait(act, "mean", t + 1)
                act.activation(rstd[0:m, i], msq[0:m, i], ACT.Exp, scale=-0.5).then_inc(norm.rstd, 1)

            def norm_high(norm, t):
                c0, m = tile_cols(t)
                for h in range(2):
                    norm.wait(act, "turned", 2 * t + h + 1)
                    act.activation(xt_hi[:, 4 * h:4 * h + 4, c0:c0 + m],
                                   ps[:, 4 + 2 * (t % 2) + h, :].rearrange("p (k c) -> p k c", k=4)[:, :, 0:m],
                                   ACT.Copy).then_inc(norm.hi, 1)

            act.wait_ge(consts_ready, 12)
            for b in range(2):
                mix, ffn, n1, n2, nf = mixes[b], ffns[b], first[b], second[b], final[b]
                prep = units(b)
                nt, nch, ncol = TILES[b], len(CHUNKS[b]), NCOL[b]
                act.preload_act_table_set("natural_log_exp_and_others")
                for t in range(nt):
                    m = tile_cols(t)[1]
                    n1.wait(act, "turned", 2 * (t - 1))
                    if b == 1:
                        act.wait_ge(stored[t % 2], 16 * (TILES[0] // 2))
                        final[0].wait(act, "scaled", TILES[0])
                    n1.wait(act, f"loaded{t % 2}", 16 * (t // 2 + 1))
                    norm_rstd(n1, t, x_in[0:m, t % 2, :])
                    if t:
                        norm_high(n1, t - 1)
                    for u in prep.get(("norm1", t), []):
                        high_unit(act, u, (ffns[0].down_done, 2 * TILES[0] * NF) if b == 1 else None)
                norm_high(n1, nt - 1)
                if b == 1:
                    act.wait_ge(ffns[0].down_done, 2 * TILES[0] * NF)
                act.preload_act_table(ACT.Silu)
                g = 0
                for n, (_, s, stage, i) in enumerate(Z_UNITS):
                    for c0, w in CHUNKS[b]:
                        act.wait_ge(mix.z_done, g + 1)
                        src = ps[:, g % 4, 0:w]
                        if n < 4:
                            act.activation(gla_y[:, n, c0:c0 + w], src, ACT.Silu).then_inc(mix.z_read, 1)
                        elif n < 8:
                            act.activation(qk[:, n - 4, c0:c0 + w], src, ACT.Copy,
                                           scale=HK ** -0.5 if n < 6 else 1.0).then_inc(mix.z_read, 1)
                        else:
                            act.activation(gate_in[:, c0:c0 + w], ps[0:RANK, g % 4, 0:w], ACT.Copy).then_inc(mix.z_read, 1)
                        g += 1
                    for u in prep["z", n]:
                        high_unit(act, u)
                for t in range(nt):
                    m = tile_cols(t)[1]
                    act.wait_ge(mix.z_done, g + 1)
                    act.activation(v_tok[0:m, t, :], ps[0:m, g % 4, :], ACT.Copy).then_inc(mix.z_read, 1)
                    g += 1
                for u in prep["v", 0]:
                    high_unit(act, u)

                def log_gate(t):
                    m = tile_cols(t)[1]
                    s = soft[0:m, :]
                    act.wait_ge(mix.pre_b, t + 1)
                    act.activation(s, lg[0:m, :], ACT.Abs).then_inc(mix.soft, 1)
                    act.wait_ge(mix.soft, 3 * t + 1)
                    act.activation(s, s, ACT.Exp, scale=-1.0).then_inc(mix.soft, 1)
                    act.wait_ge(mix.soft, 3 * t + 2)
                    act.activation(s, s, ACT.Ln, bias=1.0).then_inc(mix.soft, 1)

                def gate_exps(t):
                    m = tile_cols(t)[1]
                    b_ps = ps[:, B_GATE, 0:2 * P].rearrange("p (q c) -> p q c", q=2)
                    act.wait_ge(mix.cum, t + 1)
                    wait(act, mix.dist, t)
                    act.activation(b_cum[:, :, 0:m], b_ps[:, :, 0:m], ACT.Copy)
                    act.activation(q_exp[0:HK, :, 0, 0:m], b_ps[0:HK, :, 0:m], ACT.Exp, scale=1 / TAU)
                    act.activation(q_exp[HK:P, :, 1, 0:m], b_ps[HK:P, :, 0:m], ACT.Exp, scale=1 / TAU)
                    wait(act, mix.state0, t)
                    wait(act, mix.state1, t)
                    act.activation(decay[:, :, 0:m // CHUNK], b_ps[:, :, CHUNK - 1:m:CHUNK], ACT.Exp, scale=1 / TAU)
                    act.activation(k_exp[:, :, 0:m], b_ps[:, :, 0:m], ACT.Exp, scale=-1 / TAU).then_inc(mix.cum_read, 1)

                def k_end_exp(t):
                    m = tile_cols(t)[1]
                    act.wait_ge(mix.dist, t + 1)
                    act.activation(k_end[:, :, 0:m], k_end[:, :, 0:m], ACT.Exp, scale=-1 / TAU).then_inc(mix.k_end_exp, 1)

                def turned_copy(t):
                    m = tile_cols(t)[1]
                    act.wait_ge(mix.turned, t + 1)
                    for c in range(m // CHUNK):
                        r = slice(c * CHUNK, (c + 1) * CHUNK)
                        last = act.activation(k_end_t[r, c, :], ps[r, B_GATE, 0:2 * P], ACT.Copy)
                    last.then_inc(mix.turned_read, 1)

                def o_square(t):
                    m = tile_cols(t)[1]
                    act.wait_ge(mix.d2 if m > CHUNK else mix.d1, t + 1)
                    wait(act, mix.gla_y, t)
                    act.activation(o_sq[:, :, 0:m], ps[:, B_O, :].rearrange("p (h c) -> p h c", h=HEADS)[:, :, 0:m],
                                   ACT.Square).then_inc(mix.o_squared, 1)

                def o_rs(t):
                    m = tile_cols(t)[1]
                    act.wait_ge(mix.o_mean, t + 1)
                    act.activation(o_sq[:, :, 0:m], ps[:, B_DS, 0:HEADS * m].rearrange("p (h c) -> p h c", h=HEADS), ACT.Ln,
                                   scale=1 / HV, bias=eps_t[:, :]).then_inc(mix.o_rs, 1)
                    act.wait_ge(mix.o_rs, 2 * t + 1)
                    act.activation(o_sq[:, :, 0:m], o_sq[:, :, 0:m], ACT.Exp, scale=-0.5).then_inc(mix.o_rs, 1)

                act.preload_act_table_set("natural_log_exp_and_others")
                act.wait_ge(mix.zeros, 3)
                log_gate(0)
                gate_exps(0)
                k_end_exp(0)
                turned_copy(0)
                for j in range(CJ):
                    for ev in conv_events(b):
                        if ev[0] == "G":
                            _, m, c = ev
                            c0, w = CHUNKS[b][c]
                            gi = (3 * j + m) * nch + c
                            if m == 0:
                                act.wait_ge(mix.c_done, gi + 1)
                                act.activation(conv_y[:, j, c0:c0 + w], ps[:, gi % 3, 0:w], ACT.Copy).then_inc(mix.cg_read, 1)
                            if c == nch - 1:
                                for u in prep["conv", j, m]:
                                    high_unit(act, u, (mix.c_done, gi + 1))
                            continue
                        t = 2 * j + ev[1]
                        more = t + 1 < nt
                        if ev[0] == "X" and more:
                            log_gate(t + 1)
                        if ev[0] == "Y":
                            o_square(t)
                            if more:
                                gate_exps(t + 1)
                                k_end_exp(t + 1)
                        if ev[0] == "Z":
                            o_rs(t)
                            if more:
                                turned_copy(t + 1)
                if b == 1:
                    o_square(nt - 1)
                    o_rs(nt - 1)
                act.wait_ge(mix.c_done, 3 * CJ * nch)
                act.wait_ge(mix.gla_y, nt)
                for n in range(HEADS):
                    act.activation(xt_hi[:, HEADS + n, 0:ncol], gla_y[:, n, 0:ncol], ACT.Copy).then_inc(mix.y_hi, 1)
                act.wait_ge(mix.y_done, CJ * nch)
                for c, (c0, w) in enumerate(CHUNKS[b]):
                    wait(act, mix.cmean, c)
                    act.activation(conv_sq[:, :, 0:w], conv_y[:, :, c0:c0 + w], ACT.Square).then_inc(mix.csq, 1)
                    act.wait_ge(mix.cmean, c + 1)
                    act.activation(rs_conv[:, c0:c0 + w], ps[:, 4 + c, 0:w], ACT.Ln, scale=1 / D_CONV,
                                   bias=eps_t[:, :]).then_inc(mix.crs_step, 1)
                    act.wait_ge(mix.crs_step, c + 1)
                    act.activation(rs_conv[:, c0:c0 + w], rs_conv[:, c0:c0 + w], ACT.Exp, scale=-0.5).then_inc(mix.crs, 1)
                for n in range(CJ):
                    act.wait_ge(mix.cy, n + 1)
                    act.activation(xt_hi[:, n, 0:ncol], conv_y[:, n, 0:ncol], ACT.Copy).then_inc(mix.y_hi, 1)
                for p in range(3):
                    for u in prep["out", p]:
                        high_unit(act, u, (mix.out_done, 2 * nt * (p + 1)))
                for t in range(nt + 2):
                    if t < nt:
                        m = tile_cols(t)[1]
                        n2.wait(act, "turned", 2 * (t - 1))
                        act.wait_ge(mix.out_read, 6 * nt + 2 * (t + 1))
                        norm_rstd(n2, t, resid[0:m, t, :])
                    if t >= 2:
                        norm_high(n2, t - 2)

                def at_column(t, first_slot, col):
                    return t[:, first_slot:first_slot + 2, bass.ds(col, 1)].rearrange("p a b -> p (a b)")

                def ffn_step(f, par, pair, nxt):
                    for m in range(2):
                        for c, (c0, n) in enumerate(CHUNKS[b]):
                            if m == 0 and c == 1:
                                high_unit(act, down_unit(b, f, par, pair))
                            g = f * (2 * nch) + (m * nch + c)
                            gs = (par * 2 + m) * nch + c
                            src = ps[:, gs % 4, :]
                            i = f * nch + c
                            first_f = isinstance(f, int) and f == 0
                            act.wait_ge(ffn.up_done, g + 1)
                            if not first_f:
                                act.wait_ge(ffn.conv_done, g - 2 * nch + (1 if c == nch - 1 else 2))
                            col = m * NF + f
                            if m == 0:
                                if not first_f:
                                    act.wait_ge(ffn.h_done, i - nch + 1)
                                dst = up_a[:, c0:c0 + n]
                            else:
                                if not (first_f and c < 2):
                                    act.wait_ge(ffn.h_lo, i - 1)
                                dst = up_g[:, (par * nch + c) % 2, 0:n]
                            k = min(c0 + n, BT) - c0
                            act.activation(up_u[:, m, 2 + c0:2 + c0 + k], src[:, 0:k], ACT.Copy)
                            if k < n:
                                act.activation(up_u[:, m, 2 + BT + GAP:2 + c0 + n], src[:, k + GAP:n], ACT.Copy)
                            if b == 1 and c == 0:
                                act.activation(up_u[:, m, 0:2], at_column(ffn_half, 0, col), ACT.Copy)
                            if c == nch - 1:
                                act.activation(at_column((ffn_half, ffn_tail)[b], 0, col), src[:, BT - 2 - c0:BT - c0], ACT.Copy)
                                if b == 1:
                                    act.activation(at_column(ffn_tail_s, 0, col), src[:, ncol - 2 - c0:ncol - c0], ACT.Copy)
                                    act.activation(up_u[:, m, 2 + BT:2 + BT + GAP], at_column(params, FFN_PREV, col), ACT.Copy)
                            act.activation(dst, src[:, 0:n], ACT.Copy,
                                           scale=params[:, FFN_TAP + 2, bass.ds(col, 1)]).then_inc(ffn.up_read, 1)
                            if m == 1:
                                act.wait_ge(ffn.conv_done, g + 1)
                                act.activation(dst, dst, ACT.Silu).then_inc(ffn.silu, 1)
                                act.wait_ge(ffn.h_done, i + 1)
                                act.activation(hid_hi[:, par, c0:c0 + n], dst, ACT.Copy).then_inc(ffn.h_hi, 1)
                        if nxt is not None:
                            high_unit(act, nxt(m))

                act.preload_act_table(ACT.Silu)
                if b == 0:
                    act.wait_ge(ffn.up_done, 1)
                    act.activation(up_u[:, :, 0:2], zeros4[:, :, :], ACT.Copy)
                ffn_step(0, 0, 0, lambda m: up_unit(b, m, 1))
                with act.Fori(0, (NF - 2) // 2) as i:
                    for d in range(2):
                        f = i * 2 + (1 + d)
                        ffn_step(f, (1 + d) % 2, i + (1 + d) // 2, lambda m, f=f: up_unit(b, m, f + 1))
                ffn_step(NF - 1, (NF - 1) % 2, (NF - 1) // 2, (lambda m: prep["last", m][0]) if b == 0 else None)
                act.preload_act_table_set("natural_log_exp_and_others")
                for t in range(nt):
                    m = tile_cols(t)[1]
                    act.wait_ge(ffn.bank_free, 4 + 2 * nt * (NF - 1) + 2 * (t + 1))
                    if t >= 2:
                        act.wait_ge(stored[t % 2], 16 * ((TILES[0] // 2 if b else 0) + t // 2))
                    norm_rstd(nf, t, resid[0:m, t, :])

        @block.tensor
        def _(pe):
            def product(out, pairs):
                last = None
                for n, (lh, ll, rh, rl) in enumerate(pairs):
                    end = n == len(pairs) - 1
                    pe.matmul(out, lh, rh, start=(n == 0), stop=False)
                    pe.matmul(out, ll, rh, start=False, stop=False)
                    last = pe.matmul(out, lh, rl, start=False, stop=end)
                return last

            def columns(s, bank, c0, w):
                return product(ps[:, bank, 0:w], [
                    (w_hi[:, s, k * P:(k + 1) * P], w_lo[:, s, k * P:(k + 1) * P],
                     xt_hi[:, k, c0:c0 + w], xt_lo[:, k, c0:c0 + w]) for k in range(KT)])

            def norm_turn(norm, t):
                m = tile_cols(t)[1]
                norm.wait(pe, "scaled", t + 1)
                for h in range(2):
                    norm.wait(pe, "lo", 2 * (t - 2) + h + 1)
                    for k in range(4):
                        last = pe.transpose(ps[:, 4 + 2 * (t % 2) + h, k * P:k * P + m],
                                            x_n[0:m, t % 2, (4 * h + k) * P:(4 * h + k + 1) * P], ident[0:m, 0:m])
                    last.then_inc(norm.turned, 1)

            pe.wait_ge(consts_ready, 12)
            pe.wait_ge(rows_ready, 16 * 12)
            for i in range(12):
                last = pe.transpose(ps[:, i // 6, (i % 6) * 2 * NF:(i % 6 + 1) * 2 * NF], rows[:, i, :],
                                    ident[0:2 * NF, 0:2 * NF])
            last.then_inc(rows_turned, 1)

            for b in range(2):
                mix, ffn, n1, n2, nf = mixes[b], ffns[b], first[b], second[b], final[b]
                nt, nch, ncol = TILES[b], len(CHUNKS[b]), NCOL[b]
                for t in range(nt):
                    norm_turn(n1, t)
                if b == 1:
                    pe.wait_ge(ffns[0].up_read, 2 * len(CHUNKS[0]) * NF)
                else:
                    pe.wait_ge(params_ready, 2)
                g = 0
                for n, (_, s, stage, i) in enumerate(Z_UNITS):
                    pe.wait_ge(lo_ready[s], unit_index(b, stage, s, i) + 1)
                    for c, (c0, w) in enumerate(CHUNKS[b]):
                        wait(pe, mix.z_read, g - 3)
                        if n == 0:
                            n1.wait(pe, "lo", 2 * last_tile_of(b, c) + 2)
                        columns(s, g % 4, c0, w).then_inc(mix.z_done, 1)
                        g += 1
                for h in range(HEADS):
                    pe.wait_ge(lo_ready[h], unit_index(b, "v", h, 0) + 1)
                for t in range(nt):
                    c0, m = tile_cols(t)
                    wait(pe, mix.z_read, g - 3)
                    product(ps[0:m, g % 4, :], [
                        (xt_hi[:, k, c0:c0 + m], xt_lo[:, k, c0:c0 + m],
                         w_hi[:, :, k * P:(k + 1) * P], w_lo[:, :, k * P:(k + 1) * P]) for k in range(KT)]).then_inc(mix.z_done, 1)
                    g += 1
                pe.wait_ge(mix.z_read, g)
                if b == 0:
                    pe.wait_ge(small_ready, 48)

                def gate_product(t):
                    c0, m = tile_cols(t)
                    wait(pe, mix.turned_read, t)
                    pe.matmul(ps[0:m, B_GATE, 0:2 * P], gate_in[:, c0:c0 + m], w_al[:, :], start=True, stop=True).then_inc(mix.pre, 1)

                def gate_sums(t):
                    m = tile_cols(t)[1]
                    pe.wait_ge(mix.lg, t + 1)
                    for q in range(2):
                        last = pe.matmul(ps[:, B_GATE, q * P:q * P + m], lg[0:m, q * P:(q + 1) * P], tri[0:m, 0:m], start=True, stop=True)
                    last.then_inc(mix.cum, 1)

                def scores(t):
                    m = tile_cols(t)[1]
                    pe.wait_ge(mix.qk_exp, t + 1)
                    wait(pe, mix.att_read, t)
                    for h in range(HEADS):
                        last = pe.matmul(ps[0:m, B_ATT, h * P:h * P + m], k_exp[:, h // 2, 0:m], q_exp[:, h // 2, h % 2, 0:m],
                                         start=True, stop=True)
                    last.then_inc(mix.att_done, 1)
                    for q in range(2):
                        last = pe.transpose(ps[0:m, B_GATE, q * P:(q + 1) * P], k_end[:, q, 0:m], ident[:, :])
                    last.then_inc(mix.turned, 1)

                def outputs_1(t):
                    m = tile_cols(t)[1]
                    s = gla_s if t < BT // P else gla_s_smp
                    pe.wait_ge(mix.turned_read, t + 1)
                    pe.wait_ge(mix.att_read, t + 1)
                    wait(pe, mix.o_rs, 2 * t)
                    wait(pe, mix.state0, t)
                    wait(pe, mix.state1, t)
                    wait(pe, mix.gla_y, t)
                    for c in range(m // CHUNK):
                        for q in range(2):
                            pe.matmul(ps[:, B_DS + c, q * 2 * HV:(q + 1) * 2 * HV], k_end_t[0:m, c, q * P:(q + 1) * P],
                                      v_tok[0:m, t, q * 2 * HV:(q + 1) * 2 * HV], start=True, stop=True)
                    for h in range(HEADS):
                        pe.matmul(ps[:, B_O, h * P:h * P + m], v_tok[0:m, t, h * HV:(h + 1) * HV], att[0:m, h, 0:m],
                                  start=(h == 0), stop=False, skip_group_check=True)
                    for h in range(HEADS):
                        last = pe.matmul(ps[:, B_O, h * P:h * P + CHUNK], s[:, h // 2, :], q_exp[:, h // 2, h % 2, 0:CHUNK],
                                         start=False, stop=(m == CHUNK), skip_group_check=True)
                    last.then_inc(mix.d1, 1)

                def outputs_2(t):
                    pe.wait_ge(mix.state0, t + 1)
                    for h in range(HEADS):
                        last = pe.matmul(ps[:, B_O, h * P + CHUNK:(h + 1) * P], gla_s[:, h // 2, :],
                                         q_exp[:, h // 2, h % 2, CHUNK:P], start=False, stop=True, skip_group_check=True)
                    last.then_inc(mix.d2, 1)

                def mean_squares(t):
                    m = tile_cols(t)[1]
                    pe.wait_ge(mix.o_squared, t + 1)
                    pe.wait_ge(mix.state0, t + 1)
                    pe.matmul(ps[:, B_DS, 0:HEADS * m].rearrange("p (h c) -> p h c", h=HEADS), ones[:, :], o_sq[:, :, 0:m],
                              start=True, stop=True).then_inc(mix.o_mean, 1)

                gate_product(0)
                gate_sums(0)
                scores(0)
                for j in range(CJ):
                    for ev in conv_events(b):
                        if ev[0] == "G":
                            _, m, c = ev
                            c0, w = CHUNKS[b][c]
                            gi = (3 * j + m) * nch + c
                            if c == 0:
                                pe.wait_ge(lo_ready[m], unit_index(b, "conv", m, j) + 1)
                            if gi >= 3:
                                pj, pm, pc = (gi - 3) // (3 * nch), (gi - 3) // nch % 3, (gi - 3) % nch
                                pe.wait_ge((mix.cg_read, mix.u_done, mix.y_done)[pm], pj * nch + pc + 1)
                            columns(m, gi % 3, c0, w).then_inc(mix.c_done, 1)
                            continue
                        t = 2 * j + ev[1]
                        more = t + 1 < nt
                        if ev[0] == "X":
                            outputs_1(t)
                            if more:
                                gate_product(t + 1)
                        if ev[0] == "Y":
                            outputs_2(t)
                            if more:
                                gate_sums(t + 1)
                        if ev[0] == "Z":
                            mean_squares(t)
                            if more:
                                scores(t + 1)
                if b == 1:
                    outputs_1(nt - 1)
                    mean_squares(nt - 1)
                pe.wait_ge(mix.u_done, CJ * nch)
                pe.wait_ge(mix.y_done, CJ * nch)
                n = 0
                for p in range(4):
                    ks = [(2 * p + i + HEADS) % KT for i in range(2)]
                    ss = [(2 * p + i) % SLOTS for i in range(2)]
                    for i in range(2):
                        pe.wait_ge(lo_ready[ss[i]], unit_index(b, "out", ss[i], (2 * p + i) // SLOTS) + 1)
                    pe.wait_ge(mix.y_lo, 2 * p + 2)
                    for t in range(nt):
                        c0, m = tile_cols(t)
                        for h in range(2):
                            wait(pe, mix.out_read, n - 3)
                            product(ps[0:m, n % 4, :], [
                                (xt_hi[:, k, c0:c0 + m], xt_lo[:, k, c0:c0 + m],
                                 w_hi[:, s, h * 512:(h + 1) * 512], w_lo[:, s, h * 512:(h + 1) * 512])
                                for k, s in zip(ks, ss)]).then_inc(mix.out_done, 1)
                            n += 1
                        if p == 0 and t % 3 == 2 and t // 3 < nch:
                            c = t // 3
                            pe.wait_ge(mix.csq, c + 1)
                            for j in range(CJ):
                                last = pe.matmul(ps[:, 4 + c, 0:CHUNKS[b][c][1]], ones[:, :], conv_sq[:, j, 0:CHUNKS[b][c][1]],
                                                 start=(j == 0), stop=(j == CJ - 1))
                            last.then_inc(mix.cmean, 1)
                        if p == 3 and t >= 2:
                            norm_turn(n2, t - 2)
                for t in range(nt - 2, nt):
                    norm_turn(n2, t)
                pe.wait_ge(mix.out_read, 8 * nt)

                def down(f, par, pair, share):
                    for n in share:
                        t, h = n // 2, n % 2
                        c0, m = tile_cols(t)
                        if n == 0:
                            pe.wait_ge(lo_ready[2 + par], unit_index(b, "ffn", 2 + par, 0) + pair + 1)
                        if h == 0:
                            pe.wait_ge(ffn.h_lo, f * nch + (chunk_of_end(b, t) + 1))
                        bank = 4 + (par * 2 * nt + n) % 4
                        pe.wait_ge(ffn.bank_free, f * (2 * nt) + (n + 1))
                        s = slice(h * 512, (h + 1) * 512)
                        product(ps[0:m, bank, :], [(hid_hi[:, par, c0:c0 + m], hid_lo[:, par, c0:c0 + m],
                                                    w_hi[:, 2 + par, s], w_lo[:, 2 + par, s])]).then_inc(ffn.down_done, 1)

                def ffn_step(f, par, pair):
                    first_f = isinstance(f, int) and f == 0
                    for m in range(2):
                        pe.wait_ge(lo_ready[m], unit_index(b, "ffn", m, 0) + f + 1)
                        for c, (c0, n) in enumerate(CHUNKS[b]):
                            slot = m * nch + c
                            g = f * (2 * nch) + slot
                            if not (first_f and slot < 4):
                                pe.wait_ge(ffn.up_read, g - 3)
                            if first_f and m == 0:
                                n2.wait(pe, "lo", 2 * last_tile_of(b, c) + 2)
                            columns(m, (par * 2 * nch + slot) % 4, c0, n).then_inc(ffn.up_done, 1)
                            if not first_f:
                                down(f - 1, 1 - par, pair + (par - 1), down_share(b, slot))

                ffn_step(0, 0, 0)
                with pe.Fori(0, (NF - 2) // 2) as i:
                    for d in range(2):
                        ffn_step(i * 2 + (1 + d), (1 + d) % 2, i + (1 + d) // 2)
                ffn_step(NF - 1, (NF - 1) % 2, (NF - 1) // 2)
                down(NF - 1, (NF - 1) % 2, (NF - 1) // 2, range(2 * nt))
            for i in range(8):
                src = (ffn_tail, ffn_tail_s, conv_tail, conv_tail_s)[i // 2]
                w = 2 * NF if i < 4 else CJ
                last = pe.transpose(ps[0:w, i // 4, (i % 4) * P:(i % 4 + 1) * P], src[:, i % 2, :], ident[:, :])
                if i % 4 == 3:
                    last.then_inc(tails_turned, 1)

        @block.vector
        def _(dve):
            for h in range(2):
                dve.wait_ge(rows_turned, 1)
                dve.tensor_copy(params[:, 6 * h:6 * h + 6, :].rearrange("p a f -> p (a f)"), ps[:, h, 0:12 * NF]).then_inc(params_ready, 1)
            dve.wait_ge(params_ready, 2)

            def norm_scale(norm, t, src):
                m = tile_cols(t)[1]
                norm.wait(dve, "rstd", t + 1)
                dve.scalar_tensor_tensor(x_n[0:m, t % 2, :], src, rstd[0:m, t % 2:t % 2 + 1], gain[0:m, :],
                                         ALU.mult, ALU.mult).then_inc(norm.scaled, 1)

            def norm_low(norm, t):
                c0, m = tile_cols(t)
                for h in range(2):
                    norm.wait(dve, "hi", 2 * t + h + 1)
                    k = slice(4 * h, 4 * h + 4)
                    dve.tensor_tensor(xt_lo[:, k, c0:c0 + m],
                                      ps[:, 4 + 2 * (t % 2) + h, :].rearrange("p (k c) -> p k c", k=4)[:, :, 0:m],
                                      xt_hi[:, k, c0:c0 + m].bitcast(F32), ALU.subtract).then_inc(norm.lo, 1)

            for b in range(2):
                mix, ffn, n1, n2, nf = mixes[b], ffns[b], first[b], second[b], final[b]
                nt, nch, ncol = TILES[b], len(CHUNKS[b]), NCOL[b]
                dve.wait_ge(gain_ready, 16 * (3 * b + 1))
                for t in range(nt):
                    m = tile_cols(t)[1]
                    norm_scale(n1, t, x_in[0:m, t % 2, :])
                    if t:
                        norm_low(n1, t - 1)
                norm_low(n1, nt - 1)
                if b == 0:
                    dve.wait_ge(small_ready, 48)
                dve.wait_ge(mix.zeros, 3)

                def pre_gate(t):
                    m = tile_cols(t)[1]
                    dve.wait_ge(mix.pre, t + 1)
                    wait(dve, mix.cum, t)
                    dve.tensor_tensor(lg[0:m, :], ps[0:m, B_GATE, 0:2 * P], b_al[0:m, :], ALU.add).then_inc(mix.pre_b, 1)

                def log_gate(t):
                    m = tile_cols(t)[1]
                    dve.wait_ge(mix.soft, 3 * t + 3)
                    dve.scalar_tensor_tensor(lg[0:m, :], lg[0:m, :], 0.0, soft[0:m, :], ALU.min, ALU.subtract).then_inc(mix.lg, 1)

                def decays(t):
                    c0, m = tile_cols(t)
                    ch = m // CHUNK
                    dve.wait_ge(mix.cum_read, t + 1)
                    bv = b_cum[:, :, 0:m].rearrange("p q (c i) -> p q c i", c=ch)
                    for q in range(2):
                        last = dve.tensor_tensor(k_end[:, q, 0:m].rearrange("p (c i) -> p c i", c=ch), bv[:, q],
                                                 bv[:, q, :, CHUNK - 1:CHUNK].to_broadcast([P, ch, CHUNK]), ALU.subtract)
                    last.then_inc(mix.dist, 1)
                    dve.tensor_tensor(q_exp[0:HK, :, 0, 0:m], q_exp[0:HK, :, 0, 0:m], qk[0:HK, 0:2, c0:c0 + m], ALU.mult)
                    dve.tensor_tensor(q_exp[HK:P, :, 1, 0:m], q_exp[HK:P, :, 1, 0:m], qk[HK:P, 0:2, c0:c0 + m], ALU.mult)
                    dve.tensor_tensor(k_exp[:, :, 0:m], k_exp[:, :, 0:m], qk[:, 2:4, c0:c0 + m], ALU.mult)
                    dve.wait_ge(mix.k_end_exp, t + 1)
                    dve.tensor_tensor(k_end[:, :, 0:m], k_end[:, :, 0:m], qk[:, 2:4, c0:c0 + m], ALU.mult).then_inc(mix.qk_exp, 1)

                def masked_scores(t):
                    m = tile_cols(t)[1]
                    dve.wait_ge(mix.att_done, t + 1)
                    for h in range(HEADS):
                        last = dve.copy_predicated(att[0:m, h, 0:m], tri[0:m, 0:m].bitcast(U32), ps[0:m, B_ATT, h * P:h * P + m])
                    last.then_inc(mix.att_read, 1)

                def next_state(t, c):
                    s = gla_s if t < BT // P else gla_s_smp
                    dve.wait_ge((mix.d1, mix.d2)[c], t + 1)
                    for q in range(2):
                        for e in range(2):
                            r = slice(e * HK, (e + 1) * HK)
                            off = q * 2 * HV + e * HV
                            last = dve.scalar_tensor_tensor(s[r, q, :], s[r, q, :], decay[r, q, c:c + 1],
                                                            ps[r, B_DS + c, off:off + HV], ALU.mult, ALU.add)
                    last.then_inc((mix.state0, mix.state1)[c], 1)

                def gla_out(t):
                    c0, m = tile_cols(t)
                    dve.wait_ge(mix.o_rs, 2 * t + 2)
                    dve.scalar_tensor_tensor(o_sq[:, :, 0:m], ps[:, B_O, :].rearrange("p (h c) -> p h c", h=HEADS)[:, :, 0:m],
                                             params[:, G_GLA, 0:1], o_sq[:, :, 0:m], ALU.mult, ALU.mult).then_inc(mix.gla_step, 1)
                    dve.wait_ge(mix.gla_step, t + 1)
                    dve.tensor_tensor(gla_y[:, :, c0:c0 + m], gla_y[:, :, c0:c0 + m], o_sq[:, :, 0:m], ALU.mult).then_inc(mix.gla_y, 1)

                pre_gate(0)
                log_gate(0)
                decays(0)
                masked_scores(0)
                for j in range(CJ):
                    for ev in conv_events(b):
                        if ev[0] == "G":
                            _, m, c = ev
                            c0, w = CHUNKS[b][c]
                            gi = (3 * j + m) * nch + c
                            i = j * nch + c
                            y = conv_y[:, j, c0:c0 + w]
                            src = ps[:, gi % 3, 0:w]
                            if m == 1:
                                if c == 0:
                                    dve.tensor_copy(conv_u[:, 0:2], conv_tail[:, :, j])
                                dve.wait_ge(mix.c_done, gi + 1)
                                dve.wait_ge(mix.cg_read, i + 1)
                                dve.tensor_tensor(conv_u[:, 2 + c0:2 + c0 + w], src, y, ALU.mult).then_inc(mix.u_done, 1)
                                dve.wait_ge(mix.u_done, i + 1)
                                if c == nch - 1:
                                    dve.tensor_copy(conv_tail[:, :, j], conv_u[:, BT:BT + 2])
                                    if b == 1:
                                        dve.tensor_copy(conv_tail_s[:, :, j], conv_u[:, ncol:ncol + 2])
                                        dve.tensor_copy(conv_u[:, 2 + BT:2 + BT + GAP],
                                                        params[:, CONV_PREV:CONV_PREV + 2, j]).then_inc(mix.gap, 1)
                                        dve.wait_ge(mix.gap, j + 1)
                                for tap in (2, 1, 0):
                                    wt = params[:, CONV_TAP + tap, j:j + 1]
                                    u = conv_u[:, c0 + tap:c0 + tap + w]
                                    if tap == 2:
                                        last = dve.tensor_scalar(y, u, wt, None, ALU.mult)
                                    else:
                                        last = dve.scalar_tensor_tensor(y, u, wt, y, ALU.mult, ALU.add)
                                    last.then_inc(mix.conv_step, 1)
                                    dve.wait_ge(mix.conv_step, 3 * i + 3 - tap)
                            if m == 2:
                                dve.wait_ge(mix.c_done, gi + 1)
                                dve.tensor_tensor(y, src, y, ALU.mult).then_inc(mix.y_done, 1)
                            continue
                        t = 2 * j + ev[1]
                        more = t + 1 < nt
                        if ev[0] == "X":
                            next_state(t, 0)
                            if more:
                                pre_gate(t + 1)
                                log_gate(t + 1)
                        if ev[0] == "Y":
                            next_state(t, 1)
                            if more:
                                decays(t + 1)
                        if ev[0] == "Z":
                            if more:
                                masked_scores(t + 1)
                            gla_out(t)
                if b == 1:
                    next_state(nt - 1, 0)
                    gla_out(nt - 1)
                n_out = 0

                def conv_norm():
                    dve.wait_ge(mix.crs, nch)
                    for j in range(CJ):
                        dve.scalar_tensor_tensor(conv_y[:, j, 0:ncol], conv_y[:, j, 0:ncol], params[:, G_CONV, j:j + 1],
                                                 rs_conv[:, 0:ncol], ALU.mult, ALU.mult).then_inc(mix.cy, 1)

                for p in range(4):
                    for t in range(nt):
                        m = tile_cols(t)[1]
                        if p == 0:
                            dve.wait_ge(mix.x_in[t % 2], 16 * (t // 2 + 1))
                        for h in range(2):
                            s = slice(h * 512, (h + 1) * 512)
                            dve.wait_ge(mix.out_done, n_out + 1)
                            prev = x_in[0:m, t % 2, s] if p == 0 else resid[0:m, t, s]
                            dve.tensor_tensor(resid[0:m, t, s], ps[0:m, n_out % 4, :], prev, ALU.add).then_inc(mix.out_read, 1)
                            n_out += 1
                        if p == 0 and t == nt - 1:
                            conv_norm()
                        if p == 3:
                            if t == 0:
                                dve.wait_ge(gain_ready, 16 * (3 * b + 2))
                            if t >= 1:
                                norm_scale(n2, t - 1, resid[0:tile_cols(t - 1)[1], t - 1, :])
                            if t >= 2:
                                norm_low(n2, t - 2)
                norm_scale(n2, nt - 1, resid[0:tile_cols(nt - 1)[1], nt - 1, :])
                norm_low(n2, nt - 2)
                norm_low(n2, nt - 1)

                def add_down(f, par, share):
                    for n in share:
                        t, h = n // 2, n % 2
                        m = tile_cols(t)[1]
                        s = slice(h * 512, (h + 1) * 512)
                        dve.wait_ge(ffn.down_done, f * (2 * nt) + (n + 1))
                        dve.tensor_tensor(resid[0:m, t, s], resid[0:m, t, s], ps[0:m, 4 + (par * 2 * nt + n) % 4, :],
                                          ALU.add).then_inc(ffn.bank_free, 1)

                def ffn_step(f, par):
                    first_f = isinstance(f, int) and f == 0
                    for m in range(2):
                        for c, (c0, n) in enumerate(CHUNKS[b]):
                            slot = m * nch + c
                            g = f * (2 * nch) + slot
                            y = up_a[:, c0:c0 + n] if m == 0 else up_g[:, (par * nch + c) % 2, 0:n]
                            col = m * NF + f
                            dve.wait_ge(ffn.up_read, g + 1)
                            dve.scalar_tensor_tensor(y, up_u[:, m, c0 + 1:c0 + 1 + n], params[:, FFN_TAP + 1, bass.ds(col, 1)], y,
                                                     ALU.mult, ALU.add).then_inc(ffn.tap1, 1)
                            dve.wait_ge(ffn.tap1, g + 1)
                            dve.scalar_tensor_tensor(y, up_u[:, m, c0:c0 + n], params[:, FFN_TAP, bass.ds(col, 1)], y,
                                                     ALU.mult, ALU.add).then_inc(ffn.conv_done, 1)
                            if not first_f:
                                add_down(f - 1, 1 - par, down_share(b, slot))
                            if m == 1:
                                dve.wait_ge(ffn.silu, f * nch + (c + 1))
                                dve.tensor_tensor(y, y, up_a[:, c0:c0 + n], ALU.mult).then_inc(ffn.h_done, 1)

                dve.memset(msq[:, 0:1], 0.0).then_inc(ffn.bank_free, 4)
                ffn_step(0, 0)
                with dve.Fori(0, (NF - 2) // 2) as i:
                    for d in range(2):
                        ffn_step(i * 2 + (1 + d), (1 + d) % 2)
                ffn_step(NF - 1, (NF - 1) % 2)
                dve.wait_ge(gain_ready, 16 * (3 * b + 3))
                for t in range(nt):
                    add_down(NF - 1, (NF - 1) % 2, range(2 * t, 2 * t + 2))
                    if t:
                        norm_scale(nf, t - 1, resid[0:tile_cols(t - 1)[1], t - 1, :])
                norm_scale(nf, nt - 1, resid[0:tile_cols(nt - 1)[1], nt - 1, :])
            dve.wait_ge(tails_turned, 1)
            dve.tensor_copy(tails_out[:, 0:4, :].rearrange("p a c -> p (a c)"), ps[0:2 * NF, 0, :]).then_inc(tails_ready, 1)
            dve.wait_ge(tails_turned, 2)
            dve.tensor_copy(tails_out[0:CJ, 4:8, :].rearrange("p a c -> p (a c)"), ps[0:CJ, 1, :]).then_inc(tails_ready, 1)


_INS = ["x_prompt", "x_sample", "state_conv", "state_gla", "state_ffn_conv", "w_in", "w_alpha", "b_alpha", "conv_w",
        "g_conv", "g_gla", "w_out", "norm1", "norm2", "w_up", "ffn_conv_w", "w_down", "final_norm"]
_OUTS = [(1, SEQ, D), (1, DEC, D), (1, 1, 2, D_CONV), (1, 1, HEADS, HK, HV), (1, 1, 2, 2 * D_FF),
         (1, 1, 2, D_CONV), (1, 1, HEADS, HK, HV), (1, 1, 2, 2 * D_FF)]


def kernel(**inputs):
    import numpy as _np
    import concourse.bacc as _bacc
    from concourse.bass_utils import run_bass_kernel_spmd as _run

    nc = _bacc.Bacc("TRN2", target_bir_lowering=False, num_devices=1, dynamic_dma_scratch_size=1024)
    arrays, args = {}, []
    for name in _INS:
        a = _np.ascontiguousarray(inputs[name])
        arrays[f"in_{name}_dram"] = a
        args.append(nc.dram_tensor(f"in_{name}_dram", a.shape, mybir.dt.from_np(a.dtype), kind="ExternalInput").ap())
    for i, shape in enumerate(_OUTS):
        args.append(nc.dram_tensor(f"out_{i}_dram", shape, F32, kind="ExternalOutput").ap())
    build(nc, *args)
    r = _run(nc, [arrays], core_ids=[0])
    return tuple(r.results[0][f"out_{i}_dram"] for i in range(len(_OUTS)))
```

```python
from contextlib import ExitStack

import concourse.bass as bass
from concourse import mybir

F32 = mybir.dt.float32
F32R = mybir.dt.float32r
U32 = mybir.dt.uint32
ACT = mybir.ActivationFunctionType
ALU = mybir.AluOpType

P = 128
D = 1024
KT = D // P
SEQ = 2048
DEC = 64
D_CONV = 512
CJ = D_CONV // P
HEADS = 4
HK = 64
HV = 128
RANK = 16
TAU = 16.0
D_FF = 2816
NF = D_FF // P
EPS = 1e-6
CHUNK = 64
C_BG, C_CG, C_H = 0, D_CONV, 2 * D_CONV
C_Q = 3 * D_CONV
C_K = C_Q + HEADS * HK
C_V = C_K + HEADS * HK
C_GR = C_V + HEADS * HV
C_R = C_GR + RANK

BT = SEQ // 2
GAP = 2
NCOL = [BT, BT + GAP + DEC]
TILES = [BT // P, BT // P + 1]
CHUNKS = [[(0, 512), (512, 512)], [(0, 364), (364, 364), (728, 362)]]
Z_CHUNKS = [[(0, 256), (256, 256), (512, 512)], [(0, 256), (256, 256), (512, 290), (802, 288)]]
WMAX = NCOL[1]
SLOTS = 4

BEFORE = {
    "z": (0, 0, 0, 0), "v": (2, 2, 2, 2),
    "conv": (3, 3, 3, 3), "out": (7, 7, 7, 3), "ffn": (9, 9, 9, 5), "end": (31, 31, 20, 16),
}
FFN_TAP, FFN_PREV, CONV_TAP, CONV_PREV, G_CONV, G_GLA = 0, 3, 5, 8, 10, 11
NX = 3
T_PRODUCT, T_SUMS, T_SCORES = 0, 2, 5
TAILS_AT = 8
B_GATE, B_ATT, B_O, B_DS, B_MEAN = 3, 4, 5, 6, 7


def tile_cols(t):
    return (t * P, P) if t < BT // P else (BT + GAP, DEC)


def tile_row(b, t):
    return (b * BT + t * P, False) if t < BT // P else (0, True)


def chunk_of(b, col):
    return next(c for c, (c0, n) in enumerate(CHUNKS[b]) if col < c0 + n)


def chunk_of_end(b, t):
    return chunk_of(b, sum(tile_cols(t)) - 1)


def last_tile_of(b, chunk):
    c0, n = chunk
    return max(t for t in range(TILES[b]) if tile_cols(t)[0] < c0 + n)


def unit_index(b, stage, slot, i):
    return b * BEFORE["end"][slot] + BEFORE[stage][slot] + i


def wait(eng, sem, value):
    if isinstance(value, int) and value <= 0:
        return
    eng.wait_ge(sem, value)


def build(nc, x_prompt, x_sample, state_conv, state_gla, state_ffn, w_in, w_alpha, b_alpha, conv_w,
          g_conv, g_gla, w_out, norm1, norm2, w_up, ffn_conv_w, w_down, final_norm,
          y_prompt, y_sample, conv_prompt, gla_prompt, ffn_prompt, conv_sample, gla_sample, ffn_sample):
    with ExitStack() as ctx:
        def sem(name):
            return ctx.enter_context(nc.semaphore(name))

        def place(name, at, shape, dt=F32):
            size = 4
            for n in shape[1:]:
                size *= n
            return nc.alloc_sbuf_tensor_at(name, shape, dt, offset=at), -(-(at + size) // 32) * 32

        at = -(-nc.sbuf_base // 32) * 32
        xt_hi, at = place("xt_hi", at, [P, KT, WMAX], F32R)
        xt_lo, at = place("xt_lo", at, [P, KT, WMAX], F32R)
        w_hi, at = place("w_hi", at, [P, SLOTS, D], F32R)
        w_lo, at = place("w_lo", at, [P, SLOTS, D], F32R)
        raw, at = place("raw", at, [P, SLOTS, D])
        gain, at = place("gain", at, [P, D])
        ident, at = place("ident", at, [P, P])
        tri, at = place("tri", at, [P, P])
        ones, at = place("ones", at, [P, P])
        params, at = place("params", at, [P, 12, 2 * NF])
        zeros4, at = place("zeros4", at, [P, 2, 2])
        ffn_half, at = place("ffn_half", at, [P, 2, 2 * NF])
        ffn_tail, at = place("ffn_tail", at, [P, 2, 2 * NF])
        ffn_tail_s, at = place("ffn_tail_s", at, [P, 2, 2 * NF])
        conv_tail, at = place("conv_tail", at, [P, 2, CJ])
        conv_tail_s, at = place("conv_tail_s", at, [P, 2, CJ])
        gla_s, at = place("gla_s", at, [P, 2, HV])
        gla_s_smp, at = place("gla_s_smp", at, [P, 2, HV])
        w_al, at = place("w_al", at, [2 * RANK, 2 * P])
        w_gr, at = place("w_gr", at, [P, KT, 2 * RANK], F32R)
        b_al, at = place("b_al", at, [P, 2 * P])
        eps_t, at = place("eps_t", at, [P, 1])
        ssq, at = place("ssq", at, [P, 2])
        msq, at = place("msq", at, [P, 2])
        rstd, at = place("rstd", at, [P, 2])
        decay, at = place("decay", at, [P, 2, 2])
        resid_at = at
        resid, at = place("resid", resid_at, [P, TILES[1], D])
        qk, then = place("qk", resid_at, [P, 4, WMAX])
        v_tok, then = place("v_tok", then, [P, TILES[1], HEADS * HV])
        assert then <= at
        arena_at = at
        gla_y, at = place("gla_y", arena_at, [P, HEADS, WMAX])
        conv_y, at = place("conv_y", at, [P, CJ, WMAX])
        at_raw_gr = at - 4 * KT * RANK
        conv_u, at = place("conv_u", at, [P, 2 + WMAX])
        rs_conv, _ = place("rs_conv", at - 4384, [P, WMAX])
        free_at = at
        gate_in, at = place("gate_in", free_at, [2 * RANK, WMAX])
        lg, at = place("lg", at, [P, 2 * P])
        soft, at = place("soft", at, [P, 2 * P])
        b_cum, at = place("b_cum", at, [P, 2, P])
        q_exp, at = place("q_exp", at, [P, 2, 2, P])
        k_exp, at = place("k_exp", at, [P, 2, P])
        k_end, at = place("k_end", at, [P, 2, P])
        k_end_t, at = place("k_end_t", at, [P, HEADS, 2, HK])
        att, at = place("att", at, [P, HEADS, P])
        o_sq, at = place("o_sq", at, [P, HEADS, P])
        free_end = at
        x_in, at = place("x_in", free_at - 4 * D, [P, NX, D])
        x_n, at = place("x_n", at, [P, 2, D])
        conv_sq, _ = place("conv_sq", at - 8192, [P, CJ, 512])
        free_end = max(free_end, at)
        hid_hi, at = place("hid_hi", arena_at, [P, 2, WMAX], F32R)
        hid_lo, at = place("hid_lo", at, [P, 2, WMAX], F32R)
        squares, _ = place("squares", at, [P, 2, D])
        up_u, at = place("up_u", at, [P, 2, 2 + WMAX])
        up_a, at = place("up_a", at, [P, WMAX])
        up_g, at = place("up_g", at, [P, 2, 512])
        assert at <= free_at - 4 * D
        hid_s, at = place("hid_s", free_end, [P, 2, 2 * DEC], F32R)
        assert at <= nc.sbuf_usable_end
        raw_gr, _ = place("raw_gr", at_raw_gr, [P, KT, RANK])
        rows, _ = place("rows", arena_at, [2 * NF, 12, P])
        tails_out, _ = place("tails_out", free_at, [2 * NF, 8, P])

        ps = ctx.enter_context(nc.psum_tensor("ps", [P, 8, 512], F32))

        raw_ready = [sem(f"raw_ready{s}") for s in range(SLOTS)]
        hi_ready = [sem(f"hi_ready{s}") for s in range(SLOTS)]
        lo_ready = [sem(f"lo_ready{s}") for s in range(SLOTS)]
        rows_zero, rows_ready, consts_ready, small_ready = sem("rows_zero"), sem("rows_ready"), sem("consts_ready"), sem("small_ready")
        rows_turned, params_ready = sem("rows_turned"), sem("params_ready")
        gain_ready = sem("gain_ready")
        gr_loaded, gr_high, gr_ready = sem("gr_loaded"), sem("gr_high"), sem("gr_ready")
        stored = [sem("stored0"), sem("stored1")]
        states_stored = sem("states_stored")
        tails_turned, tails_ready = sem("tails_turned"), sem("tails_ready")

        norm_sems = {name: sem(f"norm_{name}") for name in
                     ("loaded0", "loaded1", "loaded2", "squared", "mean", "rstd", "scaled", "turned", "hi", "lo")}

        class Norm:

            def __init__(self, b, kind):
                self.loaded = [norm_sems[f"loaded{i}"] for i in range(NX)]
                self.squared = norm_sems["squared"]
                self.mean = norm_sems["mean"]
                self.rstd = norm_sems["rstd"]
                self.scaled = norm_sems["scaled"]
                self.turned = norm_sems["turned"]
                self.hi = norm_sems["hi"]
                self.lo = norm_sems["lo"]
                order = [(0, 0), (0, 1), (1, 0), (0, 2), (1, 1), (1, 2)]
                done = sum(TILES[blk] for blk, _ in order[:order.index((b, kind))])
                turned = 2 * TILES[0] * b + kind * TILES[b]
                self.base = {"squared": done, "mean": done, "rstd": done, "scaled": done,
                             "turned": 2 * turned, "hi": 2 * turned, "lo": 2 * turned}
                for i in range(NX):
                    self.base[f"loaded{i}"] = 16 * b * len(range(i, TILES[0], NX))

            def wait(self, eng, name, value):
                if value > 0:
                    eng.wait_ge(norm_sems[name], self.base[name] + value)

        class Mix:

            def __init__(self, b):
                self.z_done = sem(f"z_done_{b}")
                self.z_read = sem(f"z_read_{b}")
                self.zeros = sem(f"zeros_{b}")
                self.c_done = sem(f"c_done_{b}")
                self.cg_read = sem(f"cg_read_{b}")
                self.u_done = sem(f"u_done_{b}")
                self.conv_step = sem(f"conv_step_{b}")
                self.y_done = sem(f"y_done_{b}")
                self.pre = sem(f"pre_{b}")
                self.pre_b = sem(f"pre_b_{b}")
                self.soft = sem(f"soft_{b}")
                self.lg = sem(f"lg_{b}")
                self.cum = sem(f"cum_{b}")
                self.cum_read = sem(f"cum_read_{b}")
                self.dist = sem(f"dist_{b}")
                self.k_end_exp = sem(f"k_end_exp_{b}")
                self.qk_exp = sem(f"qk_exp_{b}")
                self.att_done = sem(f"att_done_{b}")
                self.att_read = sem(f"att_read_{b}")
                self.turned = sem(f"turned_{b}")
                self.turned_read = sem(f"turned_read_{b}")
                self.d1 = sem(f"d1_{b}")
                self.d2 = sem(f"d2_{b}")
                self.state0 = sem(f"state0_{b}")
                self.state1 = sem(f"state1_{b}")
                self.o_squared = sem(f"o_squared_{b}")
                self.o_mean = sem(f"o_mean_{b}")
                self.o_rs = sem(f"o_rs_{b}")
                self.gla_step = sem(f"gla_step_{b}")
                self.gla_y = sem(f"gla_y_{b}")
                self.y_hi = sem(f"y_hi_{b}")
                self.y_lo = sem(f"y_lo_{b}")
                self.y_lo_first = sem(f"y_lo_first_{b}")
                self.csum = sem(f"csum_{b}")
                self.csq = sem(f"csq_{b}")
                self.cmean = sem(f"cmean_{b}")
                self.crs_step = sem(f"crs_step_{b}")
                self.crs = sem(f"crs_{b}")
                self.cy = sem(f"cy_{b}")
                self.out_done = sem(f"out_done_{b}")
                self.out_read = sem(f"out_read_{b}")
                self.gap = sem(f"gap_{b}")
                self.x_in = [sem(f"x_again0_{b}"), sem(f"x_again1_{b}")]

        class Ffn:

            def __init__(self, b):
                self.up_done = sem(f"up_done_{b}")
                self.up_read = sem(f"up_read_{b}")
                self.tap1 = sem(f"tap1_{b}")
                self.conv_done = sem(f"conv_done_{b}")
                self.silu = sem(f"silu_{b}")
                self.h_done = sem(f"h_done_{b}")
                self.h_hi = sem(f"h_hi_{b}")
                self.h_lo = sem(f"h_lo_{b}")
                self.half = sem(f"down_half_{b}")
                self.down_done = sem(f"down_done_{b}")
                self.bank_free = sem(f"bank_free_{b}")

        first = [Norm(b, 0) for b in range(2)]
        second = [Norm(b, 1) for b in range(2)]
        final = [Norm(b, 2) for b in range(2)]
        mixes = [Mix(b) for b in range(2)]
        ffns = [Ffn(b) for b in range(2)]

        w_in_v = w_in[0].rearrange("(k p) c -> p k c", p=P)
        w_up_v = w_up[0].rearrange("(k p) c -> p k c", p=P)

        def x_rows(b, t):
            r, smp = tile_row(b, t)
            return (x_sample if smp else x_prompt)[0, r:r + tile_cols(t)[1], :]

        def y_rows(b, t):
            r, smp = tile_row(b, t)
            return (y_sample if smp else y_prompt)[0, r:r + tile_cols(t)[1], :]

        def in_unit(c0):
            return w_in_v[:, :, c0:c0 + P]

        Z_COLS = [C_R + P * u for u in range(HEADS)] + [C_Q + P * u for u in range(4)]
        NZ = len(Z_COLS)
        GATE = NZ

        def z_groups(b):
            nch = len(Z_CHUNKS[b])
            return ([(n, c) for c in range(nch) for n in range(HEADS)] + [(GATE, c) for c in range(nch)]
                    + [(n, c) for n in range(HEADS, NZ) for c in range(nch)])

        def early_tiles(b):
            return last_tile_of(b, Z_CHUNKS[b][0]) + 1

        def units(b):
            def v_unit(slot):
                src = w_in[0, 2 * slot * P:2 * (slot + 1) * P, C_V:C_V + HEADS * HV].rearrange("(k p) c -> p k c", p=P)
                return src, slot, unit_index(b, "v", slot, 0)

            def conv(j, m):
                return in_unit((C_CG, C_H, C_BG)[m] + P * j), m, unit_index(b, "conv", m, j)

            def out(n):
                k = (n + HEADS) % KT
                return w_out[0, k * P:(k + 1) * P, :], n % SLOTS, unit_index(b, "out", n % SLOTS, n // SLOTS)

            e = {}
            if b == 0:
                e["norm1", 1] = [z_unit(b, 0)]
                e["norm1", 2] = [z_unit(b, 1)]
            e["norm1", 3] = [z_unit(b, 2)]
            e["norm1", 4] = [z_unit(b, 3)]
            for n in range(NZ):
                e["z", n] = [z_unit(b, n + SLOTS) if n + SLOTS < NZ else v_unit((n + SLOTS) % SLOTS)]
            e["v", 0] = [conv(0, 0), conv(0, 1), conv(0, 2), out(3)]
            for j in range(CJ):
                for m in range(3):
                    e["conv", j, m] = [conv(j + 1, m)] if j + 1 < CJ else [out(m)]
            for p in range(2):
                e["out", p] = [out(4 + 2 * p), out(5 + 2 * p)]
            e["out", 2] = [up_unit(b, 0, 0), up_unit(b, 1, 0)]
            e["last", 0] = [z_unit(b + 1, 0)] if b == 0 else []
            e["last", 1] = [z_unit(b + 1, 1)] if b == 0 else []
            return e

        def z_unit(b, n):
            return in_unit(Z_COLS[n]), n % SLOTS, unit_index(b, "z", n % SLOTS, n // SLOTS)

        def up_unit(b, m, f):
            return w_up_v[:, :, bass.ds(m * D_FF + f * P, P)], m, unit_index(b, "ffn", m, 0) + f

        def down_unit(b, f, par, pair):
            return w_down[0, bass.ds(f * P, P), :], 2 + par, unit_index(b, "ffn", 2 + par, 0) + pair

        def load_unit(sp, unit):
            src, s, n = unit
            wait(sp, lo_ready[s], n)
            dst = raw[:, s, :]
            if len(src.shape) == 3:
                dst = dst.rearrange("p (k c) -> p k c", k=src.shape[1])
            sp.dma_start(dst, src).then_inc(raw_ready[s], 16)

        def high_unit(act, unit, used=None):
            _, s, n = unit
            wait(act, raw_ready[s], 16 * (n + 1))
            if used:
                wait(act, *used)
            act.activation(w_hi[:, s, :], raw[:, s, :], ACT.Copy).then_inc(hi_ready[s], 1)

        def low_unit(pool, unit):
            _, s, n = unit
            wait(pool, hi_ready[s], n + 1)
            pool.tensor_tensor(w_lo[:, s, :], raw[:, s, :], w_hi[:, s, :].bitcast(F32),
                               ALU.subtract).then_inc(lo_ready[s], 1)

        def conv_events(b, j):
            groups = [(m, c) for m in range(3) for c in range(len(CHUNKS[b]))]
            steps = [("X", 0), ("Y", 0), ("Z", 0), ("X", 1), ("Y", 1), ("Z", 1)]
            if 2 * (j + 1) < TILES[b] and j == CJ - 1:
                steps += [("X", 2), ("Z", 2)]
            out, g = [], 0
            for n, (step, i) in enumerate(steps):
                out.append((step, 2 * j + i))
                upto = (n + 1) * len(groups) // len(steps)
                while g < upto:
                    out.append(("G",) + groups[g])
                    g += 1
            return out

        def head_parts(b):
            return [(n, c0, w) for c0, w in CHUNKS[b] for n in range(2)] + [(n, 0, NCOL[b]) for n in range(2, HEADS)]

        def low_part(eng, n, c0, w):
            return eng.tensor_tensor(xt_lo[:, HEADS + n, c0:c0 + w], gla_y[:, n, c0:c0 + w],
                                     xt_hi[:, HEADS + n, c0:c0 + w].bitcast(F32), ALU.subtract)

        def down_share(b, slot):
            nd, ns = 2 * TILES[b], 2 * len(CHUNKS[b])
            return range(slot * nd // ns, (slot + 1) * nd // ns)

        block = ctx.enter_context(nc.Block())

        @block.sync
        def _(sp):
            def load_gain(src):
                sp.dma_start(gain[:, :], src.partition_broadcast(P)).then_inc(gain_ready, 16)

            def load_parameters():
                sp.wait_ge(rows_zero, 1)
                with nc.allow_non_contiguous_dma(reason="small parameters"):
                    for i in range(3):
                        sp.dma_start(rows[:, FFN_TAP + i, :], ffn_conv_w[0, i].rearrange("(f p) -> f p", p=P)).then_inc(rows_ready, 16)
                        sp.dma_start(rows[0:CJ, CONV_TAP + i, :], conv_w[0, i].rearrange("(f p) -> f p", p=P)).then_inc(rows_ready, 16)
                    for i in range(2):
                        sp.dma_start(rows[:, FFN_PREV + i, :], state_ffn[0, 0, i].rearrange("(f p) -> f p", p=P)).then_inc(rows_ready, 16)
                        sp.dma_start(rows[0:CJ, CONV_PREV + i, :], state_conv[0, 0, i].rearrange("(f p) -> f p", p=P)).then_inc(rows_ready, 16)
                    sp.dma_start(rows[0:CJ, G_CONV, :], g_conv[0].rearrange("(f p) -> f p", p=P)).then_inc(rows_ready, 16)
                    sp.dma_start(rows[0:1, G_GLA, :], g_gla).then_inc(rows_ready, 16)

            def store_results(b, tiles):
                for t in tiles:
                    final[b].wait(sp, "scaled", t + 1)
                    m = tile_cols(t)[1]
                    sp.dma_start(y_rows(b, t), x_n[0:m, t % 2, :]).then_inc(stored[t % 2], 16)

            for b in range(2):
                mix, ffn, n1, n2, nf = mixes[b], ffns[b], first[b], second[b], final[b]
                prep = units(b)
                nt = TILES[b]

                def load_x(t, blk):
                    m = tile_cols(t)[1]
                    sp.dma_start(x_in[0:m, t % NX, :], x_rows(blk, t)).then_inc(first[blk].loaded[t % NX], 16)

                def load_x_again(t):
                    m = tile_cols(t)[1]
                    sp.dma_start(x_in[0:m, 1 + t % 2, :], x_rows(b, t)).then_inc(mix.x_in[t % 2], 16)

                for t in range(NX * b, nt):
                    n1.wait(sp, "scaled", t - NX + 1)
                    load_x(t, b)
                    if t == 1:
                        load_gain(norm1[0])
                    if t == 2:
                        for n in (1, 2):
                            for u in prep["norm1", n]:
                                load_unit(sp, u)
                        load_parameters()
                        with nc.allow_non_contiguous_dma(reason="small parameters"):
                            sp.dma_start(raw_gr[:, :, :], w_in_v[:, :, C_GR:C_R]).then_inc(gr_loaded, 16)
                        for i in range(2):
                            sp.dma_start(w_al[i * RANK:(i + 1) * RANK, :], w_alpha[0]).then_inc(small_ready, 16)
                        sp.dma_start(b_al[:, :], b_alpha[0].partition_broadcast(P)).then_inc(small_ready, 16)
                        sp.dma_start(gla_s_smp[:, :, :], state_gla[0, 0].rearrange("(q e) k v -> (e k) q v", e=2)).then_inc(small_ready, 16)
                    for u in prep.get(("norm1", t), []) if t > 2 else []:
                        load_unit(sp, u)
                for n in range(NZ):
                    if n == SLOTS and b == 1:
                        n1.wait(sp, "scaled", nt)
                        load_gain(final_norm)
                        store_results(0, range(TILES[0]))
                    for u in prep["z", n]:
                        load_unit(sp, u)
                (final[0] if b else n1).wait(sp, "scaled", TILES[0])
                load_gain(norm2[0])
                for u in prep["v", 0]:
                    load_unit(sp, u)
                for j in range(CJ):
                    for m in range(3):
                        for u in prep["conv", j, m]:
                            load_unit(sp, u)
                if b == 1:
                    sp.wait_ge(mix.state1, nt - 1)
                    sp.wait_ge(mix.state0, nt)
                    sp.dma_start(gla_prompt[0, 0].rearrange("(q e) k v -> (e k) q v", e=2), gla_s[:, :, :]).then_inc(states_stored, 16)
                    sp.dma_start(gla_sample[0, 0].rearrange("(q e) k v -> (e k) q v", e=2), gla_s_smp[:, :, :]).then_inc(states_stored, 16)
                sp.wait_ge(mix.gla_y, nt)
                load_x_again(0)
                load_x_again(1)
                for p in range(2):
                    for u in prep["out", p]:
                        load_unit(sp, u)
                for t in range(2, nt):
                    sp.wait_ge(mix.out_read, 2 * (t - 1))
                    load_x_again(t)
                for u in prep["out", 2]:
                    load_unit(sp, u)
                load_unit(sp, down_unit(b, 0, 0, 0))
                load_unit(sp, up_unit(b, 0, 1))
                load_unit(sp, up_unit(b, 1, 1))
                n2.wait(sp, "scaled", nt)
                if b == 0:
                    load_gain(norm1[0])
                    sp.wait_ge(mix.out_read, 8 * nt)
                    for t in range(NX):
                        load_x(t, 1)
                else:
                    load_gain(final_norm)
                with sp.Fori(0, (NF - 2) // 2) as i:
                    for d in range(2):
                        f = i * 2 + (1 + d)
                        load_unit(sp, down_unit(b, f, (1 + d) % 2, i + (1 + d) // 2))
                        load_unit(sp, up_unit(b, 0, f + 1))
                        load_unit(sp, up_unit(b, 1, f + 1))
                load_unit(sp, down_unit(b, NF - 1, (NF - 1) % 2, (NF - 1) // 2))
                for m in range(2):
                    for u in prep["last", m]:
                        load_unit(sp, u)
                if b == 1:
                    store_results(1, range(TAILS_AT // 2 + 1))
                    sp.wait_ge(tails_ready, 2)
                    for i, dst in enumerate((ffn_prompt, ffn_sample)):
                        for r in range(2):
                            sp.dma_start(dst[0, 0, r].rearrange("(f p) -> f p", p=P), tails_out[:, 2 * i + r, :]).then_inc(states_stored, 16)
                    for i, dst in enumerate((conv_prompt, conv_sample)):
                        for r in range(2):
                            sp.dma_start(dst[0, 0, r].rearrange("(f p) -> f p", p=P), tails_out[0:CJ, 4 + 2 * i + r, :]).then_inc(states_stored, 16)
                    store_results(1, range(TAILS_AT // 2 + 1, nt))
            sp.wait_ge(states_stored, 16 * 10)
            for par in range(2):
                sp.wait_ge(stored[par], 16 * sum((nt + 1 - par) // 2 for nt in TILES))

        @block.gpsimd
        def _(pool):
            pool.memset(rows[:, :, :], 0.0).then_inc(rows_zero, 1)
            pool.memset(ident[:, :], 0.0).then_inc(consts_ready, 1)
            pool.memset(tri[:, :], 1.0).then_inc(consts_ready, 1)
            pool.memset(ones[:, :], 1.0).then_inc(consts_ready, 1)
            pool.memset(eps_t[:, :], EPS).then_inc(consts_ready, 1)
            pool.memset(zeros4[:, :, :], 0.0).then_inc(consts_ready, 1)
            pool.memset(conv_tail[:, :, :], 0.0).then_inc(consts_ready, 1)
            pool.memset(gla_s[:, :, :], 0.0).then_inc(consts_ready, 1)
            pool.memset(xt_hi[:, :, BT:BT + GAP].bitcast(F32), 0.0).then_inc(consts_ready, 1)
            pool.memset(xt_lo[:, :, BT:BT + GAP].bitcast(F32), 0.0).then_inc(consts_ready, 1)
            pool.wait_ge(consts_ready, 9)
            pool.affine_select(out=ident[:, :], in_=ident[:, :], compare_op=ALU.not_equal, fill=1.0, base=0,
                               pattern=[[-1, P]], channel_multiplier=1).then_inc(consts_ready, 1)
            pool.affine_select(out=tri[:, :], in_=tri[:, :], compare_op=ALU.is_ge, fill=0.0, base=0,
                               pattern=[[1, P]], channel_multiplier=-1).then_inc(consts_ready, 1)
            pool.wait_ge(consts_ready, 11)
            pool.memset(tri[0:CHUNK, CHUNK:P], 0.0).then_inc(consts_ready, 1)

            for b in range(2):
                mix, ffn, n1, n2, nf = mixes[b], ffns[b], first[b], second[b], final[b]
                prep = units(b)
                nt, nch = TILES[b], len(CHUNKS[b])
                for t in range(nt):
                    for u in prep.get(("norm1", t), []):
                        low_unit(pool, u)
                if b == 0:
                    pool.wait_ge(gr_high, 1)
                    pool.tensor_tensor(w_gr[:, :, RANK:2 * RANK], raw_gr[:, :, :], w_gr[:, :, 0:RANK].bitcast(F32),
                                       ALU.subtract).then_inc(gr_ready, 1)
                for n in range(NZ):
                    if n == SLOTS - 1:
                        n1.wait(pool, "turned", 2 * nt)
                        if b == 1:
                            for par in range(2):
                                pool.wait_ge(stored[par], 16 * (TILES[0] // 2))
                        pool.memset(q_exp[:, :, :, :], 0.0).then_inc(mix.zeros, 1)
                        pool.memset(k_end_t[:, :, :, :], 0.0).then_inc(mix.zeros, 1)
                        pool.memset(att[:, :, :], 0.0).then_inc(mix.zeros, 1)
                    for u in prep["z", n]:
                        low_unit(pool, u)
                for u in prep["v", 0]:
                    low_unit(pool, u)
                for j in range(CJ):
                    for m in range(3):
                        for u in prep["conv", j, m]:
                            low_unit(pool, u)
                for i, (n, c0, w) in enumerate(head_parts(b)):
                    if i >= 2 * nch:
                        pool.wait_ge(mix.y_hi, i + 1)
                        low_part(pool, n, c0, w).then_inc(mix.y_lo, 1)
                for n in range(CJ):
                    pool.wait_ge(mix.y_hi, len(head_parts(b)) + n + 1)
                    pool.tensor_tensor(xt_lo[:, n, 0:NCOL[b]], conv_y[:, n, 0:NCOL[b]],
                                       xt_hi[:, n, 0:NCOL[b]].bitcast(F32), ALU.subtract).then_inc(mix.y_lo, 1)
                for p in range(3):
                    for u in prep["out", p]:
                        low_unit(pool, u)

                def ffn_step(f, par, pair, nxt):
                    low_unit(pool, down_unit(b, f, par, pair))
                    if nxt is not None:
                        low_unit(pool, nxt(0))
                    for c, (c0, n) in enumerate(CHUNKS[b]):
                        i = f * nch + c
                        g = up_g[:, (par * nch + c) % 2, 0:n]
                        pool.wait_ge(ffn.h_hi, i + 1)
                        if b == 1 and c == nch - 1:
                            pool.tensor_tensor(hid_s[:, par, DEC:2 * DEC], g[:, n - DEC:n],
                                               hid_hi[:, par, c0 + n - DEC:c0 + n].bitcast(F32), ALU.subtract)
                        pool.tensor_tensor(hid_lo[:, par, c0:c0 + n], g, hid_hi[:, par, c0:c0 + n].bitcast(F32),
                                           ALU.subtract).then_inc(ffn.h_lo, 1)
                    if nxt is not None:
                        low_unit(pool, nxt(1))

                ffn_step(0, 0, 0, lambda m: up_unit(b, m, 1))
                with pool.Fori(0, (NF - 2) // 2) as i:
                    for d in range(2):
                        f = i * 2 + (1 + d)
                        ffn_step(f, (1 + d) % 2, i + (1 + d) // 2, lambda m, f=f: up_unit(b, m, f + 1))
                ffn_step(NF - 1, (NF - 1) % 2, (NF - 1) // 2, (lambda m: prep["last", m][0]) if b == 0 else None)

        @block.scalar
        def _(act):
            def norm_rstd(norm, t, src):
                m = tile_cols(t)[1]
                i = slice(t % 2, t % 2 + 1)
                act.activation(squares[0:m, t % 2, :], src, ACT.Square, accum_out=ssq[0:m, i]).then_inc(norm.squared, 1)
                norm.wait(act, "squared", t + 1)
                act.activation(msq[0:m, i], ssq[0:m, i], ACT.Ln, scale=1 / D, bias=eps_t[0:m, :]).then_inc(norm.mean, 1)
                norm.wait(act, "mean", t + 1)
                act.activation(rstd[0:m, i], msq[0:m, i], ACT.Exp, scale=-0.5).then_inc(norm.rstd, 1)

            def norm_high(norm, t):
                c0, m = tile_cols(t)
                for h in range(2):
                    norm.wait(act, "turned", 2 * t + h + 1)
                    act.activation(xt_hi[:, 4 * h:4 * h + 4, c0:c0 + m],
                                   ps[:, 4 + 2 * (t % 2) + h, :].rearrange("p (k c) -> p k c", k=4)[:, :, 0:m],
                                   ACT.Copy).then_inc(norm.hi, 1)

            act.wait_ge(consts_ready, 12)
            for b in range(2):
                mix, ffn, n1, n2, nf = mixes[b], ffns[b], first[b], second[b], final[b]
                prep = units(b)
                nt, nch, ncol = TILES[b], len(CHUNKS[b]), NCOL[b]
                groups = z_groups(b)
                n_r = HEADS * len(Z_CHUNKS[b])

                def read_group(g):
                    n, c = groups[g]
                    c0, w = Z_CHUNKS[b][c]
                    act.wait_ge(mix.z_done, g + 1)
                    src = ps[:, g % 4, 0:w]
                    if g == 0 and b == 1:
                        act.wait_ge(ffns[0].down_done, 2 * TILES[0] * NF)
                    if n < HEADS:
                        act.activation(gla_y[:, n, c0:c0 + w], src, ACT.Copy).then_inc(mix.z_read, 1)
                    elif n == GATE:
                        act.activation(gate_in[:, c0:c0 + w], ps[0:2 * RANK, g % 4, 0:w], ACT.Copy).then_inc(mix.z_read, 1)
                    else:
                        act.activation(qk[:, n - HEADS, c0:c0 + w], src, ACT.Copy,
                                       scale=HK ** -0.5 if n < HEADS + 2 else 1.0).then_inc(mix.z_read, 1)
                    if c == len(Z_CHUNKS[b]) - 1 and n != GATE:
                        for u in prep["z", n]:
                            high_unit(act, u)

                lag = 1 + b
                act.preload_act_table_set("natural_log_exp_and_others")
                g = 0
                for t in range(nt):
                    m = tile_cols(t)[1]
                    n1.wait(act, "scaled", t - 1)
                    n1.wait(act, f"loaded{t % NX}", 16 * (t // NX + 1))
                    norm_rstd(n1, t, x_in[0:m, t % NX, :])
                    if t >= lag:
                        norm_high(n1, t - lag)
                    for u in prep.get(("norm1", t), []):
                        high_unit(act, u, (ffns[0].down_done, 2 * TILES[0] * NF) if b == 1 else None)
                    if b == 0 and t == 4:
                        act.wait_ge(gr_loaded, 16)
                        act.activation(w_gr[:, :, 0:RANK], raw_gr[:, :, :], ACT.Copy).then_inc(gr_high, 1)
                    if t > early_tiles(b):
                        read_group(g)
                        g += 1
                for t in range(nt - lag, nt):
                    norm_high(n1, t)
                if b == 1:
                    for t in range(TILES[0]):
                        n1.wait(act, "scaled", nt)
                        final[0].wait(act, "scaled", t - 1)
                        norm_rstd(final[0], t, resid[:, t, :])
                        if g < n_r:
                            read_group(g)
                            g += 1
                while g < n_r:
                    read_group(g)
                    g += 1
                act.preload_act_table(ACT.Silu)
                act.wait_ge(mix.z_read, n_r)
                for n in range(HEADS):
                    act.activation(gla_y[:, n, 0:ncol], gla_y[:, n, 0:ncol], ACT.Silu)
                act.preload_act_table_set("natural_log_exp_and_others")
                if b == 1:
                    final[0].wait(act, "scaled", TILES[0])
                while g < len(groups):
                    read_group(g)
                    g += 1

                def log_gate(t):
                    m = tile_cols(t)[1]
                    s = soft[0:m, :]
                    act.wait_ge(mix.pre_b, t + 1)
                    act.activation(s, lg[0:m, :], ACT.Abs).then_inc(mix.soft, 1)
                    act.wait_ge(mix.soft, 3 * t + 1)
                    act.activation(s, s, ACT.Exp, scale=-1.0).then_inc(mix.soft, 1)
                    act.wait_ge(mix.soft, 3 * t + 2)
                    act.activation(s, s, ACT.Ln, bias=1.0).then_inc(mix.soft, 1)

                def gate_exps(t):
                    m = tile_cols(t)[1]
                    b_ps = ps[:, B_GATE, 0:2 * P].rearrange("p (q c) -> p q c", q=2)
                    act.wait_ge(mix.cum, t + 1)
                    wait(act, mix.dist, t)
                    act.activation(b_cum[:, :, 0:m], b_ps[:, :, 0:m], ACT.Copy)
                    act.activation(q_exp[0:HK, :, 0, 0:m], b_ps[0:HK, :, 0:m], ACT.Exp, scale=1 / TAU)
                    act.activation(q_exp[HK:P, :, 1, 0:m], b_ps[HK:P, :, 0:m], ACT.Exp, scale=1 / TAU)
                    wait(act, mix.state0, t)
                    wait(act, mix.state1, t)
                    act.activation(decay[:, :, 0:m // CHUNK], b_ps[:, :, CHUNK - 1:m:CHUNK], ACT.Exp, scale=1 / TAU)
                    act.activation(k_exp[:, :, 0:m], b_ps[:, :, 0:m], ACT.Exp, scale=-1 / TAU).then_inc(mix.cum_read, 1)

                def k_end_exp(t):
                    m = tile_cols(t)[1]
                    act.wait_ge(mix.dist, t + 1)
                    act.activation(k_end[:, :, 0:m], k_end[:, :, 0:m], ACT.Exp, scale=-1 / TAU).then_inc(mix.k_end_exp, 1)

                def turned_copy(t):
                    m = tile_cols(t)[1]
                    act.wait_ge(mix.turned, t + 1)
                    for c in range(m // CHUNK):
                        r = slice(c * CHUNK, (c + 1) * CHUNK)
                        last = act.activation(k_end_t[r, :, c, :], ps[r, B_GATE, 0:2 * P].rearrange("p (h k) -> p h k", h=HEADS), ACT.Copy)
                    last.then_inc(mix.turned_read, 1)

                def o_square(t):
                    m = tile_cols(t)[1]
                    act.wait_ge(mix.d2 if m > CHUNK else mix.d1, t + 1)
                    wait(act, mix.gla_y, t)
                    act.activation(o_sq[:, :, 0:m], ps[:, B_O, :].rearrange("p (h c) -> p h c", h=HEADS)[:, :, 0:m],
                                   ACT.Square).then_inc(mix.o_squared, 1)

                def o_rs(t):
                    m = tile_cols(t)[1]
                    act.wait_ge(mix.o_mean, t + 1)
                    act.activation(o_sq[:, :, 0:m], ps[:, B_MEAN, 0:HEADS * m].rearrange("p (h c) -> p h c", h=HEADS), ACT.Ln,
                                   scale=1 / HV, bias=eps_t[:, :]).then_inc(mix.o_rs, 1)
                    act.wait_ge(mix.o_rs, 2 * t + 1)
                    act.activation(o_sq[:, :, 0:m], o_sq[:, :, 0:m], ACT.Exp, scale=-0.5).then_inc(mix.o_rs, 1)

                act.wait_ge(mix.zeros, 3)
                for t in range(nt):
                    m = tile_cols(t)[1]
                    act.wait_ge(mix.z_done, g + t + 1)
                    act.activation(v_tok[0:m, t, :], ps[0:m, t % 3, :], ACT.Copy).then_inc(mix.z_read, 1)
                    if t == T_PRODUCT:
                        log_gate(0)
                    if t == T_SUMS:
                        gate_exps(0)
                        k_end_exp(0)
                    if t == T_SCORES:
                        turned_copy(0)
                for u in prep["v", 0]:
                    high_unit(act, u)
                for j in range(CJ):
                    for ev in conv_events(b, j):
                        if ev[0] == "G":
                            _, m, c = ev
                            c0, w = CHUNKS[b][c]
                            gi = (3 * j + m) * nch + c
                            if m == 0:
                                act.wait_ge(mix.c_done, gi + 1)
                                act.activation(conv_y[:, j, c0:c0 + w], ps[:, gi % 3, 0:w], ACT.Copy).then_inc(mix.cg_read, 1)
                            if c == nch - 1 and (j, m) != (CJ - 1, 2):
                                for u in prep["conv", j, m]:
                                    high_unit(act, u, (mix.c_done, gi + 1))
                            continue
                        t = ev[1]
                        more = t + 1 < nt
                        if ev[0] == "X":
                            if more:
                                log_gate(t + 1)
                            if tile_cols(t)[1] == CHUNK:
                                o_square(t)
                        if ev[0] == "Y":
                            o_square(t)
                            if more:
                                gate_exps(t + 1)
                                k_end_exp(t + 1)
                        if ev[0] == "Z":
                            o_rs(t)
                            if more:
                                turned_copy(t + 1)
                act.wait_ge(mix.gla_y, nt)
                for i, (n, c0, w) in enumerate(head_parts(b)):
                    if i == 2 * nch:
                        for u in prep["conv", CJ - 1, 2]:
                            high_unit(act, u)
                    act.wait_ge(mix.c_done, (3 * CJ - 1) * nch + chunk_of(b, c0 + w - 1) + 1)
                    act.activation(xt_hi[:, HEADS + n, c0:c0 + w], gla_y[:, n, c0:c0 + w], ACT.Copy).then_inc(mix.y_hi, 1)
                act.wait_ge(mix.y_done, CJ * nch)
                for c, (c0, w) in enumerate(CHUNKS[b]):
                    wait(act, mix.cmean, c)
                    act.activation(conv_sq[:, :, 0:w], conv_y[:, :, c0:c0 + w], ACT.Square).then_inc(mix.csq, 1)
                    act.wait_ge(mix.cmean, c + 1)
                    act.activation(rs_conv[:, c0:c0 + w], ps[:, 4 + c, 0:w], ACT.Ln, scale=1 / D_CONV,
                                   bias=eps_t[:, :]).then_inc(mix.crs_step, 1)
                    act.wait_ge(mix.crs_step, c + 1)
                    act.activation(rs_conv[:, c0:c0 + w], rs_conv[:, c0:c0 + w], ACT.Exp, scale=-0.5).then_inc(mix.crs, 1)
                for n in range(CJ):
                    act.wait_ge(mix.cy, n + 1)
                    act.activation(xt_hi[:, n, 0:ncol], conv_y[:, n, 0:ncol], ACT.Copy).then_inc(mix.y_hi, 1)
                for p in range(3):
                    for u in prep["out", p]:
                        high_unit(act, u, (mix.out_done, 2 * nt * (p + 1)))
                for t in range(nt + 2):
                    if t < nt:
                        m = tile_cols(t)[1]
                        n2.wait(act, "scaled", t - 1)
                        act.wait_ge(mix.out_read, 6 * nt + 2 * (t + 1))
                        norm_rstd(n2, t, resid[0:m, t, :])
                    if t >= 2:
                        norm_high(n2, t - 2)

                def at_column(t, first_slot, col):
                    return t[:, first_slot:first_slot + 2, bass.ds(col, 1)].rearrange("p a b -> p (a b)")

                def ffn_step(f, par, pair, nxt):
                    for m in range(2):
                        for c, (c0, n) in enumerate(CHUNKS[b]):
                            if m == 0 and c == 1:
                                high_unit(act, down_unit(b, f, par, pair))
                            g = f * (2 * nch) + (m * nch + c)
                            gs = (par * 2 + m) * nch + c
                            src = ps[:, gs % 4, :]
                            i = f * nch + c
                            first_f = isinstance(f, int) and f == 0
                            act.wait_ge(ffn.up_done, g + 1)
                            if not first_f:
                                act.wait_ge(ffn.conv_done, g - 2 * nch + (1 if c == nch - 1 else 2))
                            col = m * NF + f
                            if m == 0:
                                if not first_f:
                                    act.wait_ge(ffn.h_done, i - nch + 1)
                                dst = up_a[:, c0:c0 + n]
                            else:
                                if not (first_f and c < 2):
                                    act.wait_ge(ffn.h_lo, i - 1)
                                dst = up_g[:, (par * nch + c) % 2, 0:n]
                            k = min(c0 + n, BT) - c0
                            act.activation(up_u[:, m, 2 + c0:2 + c0 + k], src[:, 0:k], ACT.Copy)
                            if k < n:
                                act.activation(up_u[:, m, 2 + BT + GAP:2 + c0 + n], src[:, k + GAP:n], ACT.Copy)
                            if b == 1 and c == 0:
                                act.activation(up_u[:, m, 0:2], at_column(ffn_half, 0, col), ACT.Copy)
                            if c == nch - 1:
                                act.activation(at_column((ffn_half, ffn_tail)[b], 0, col), src[:, BT - 2 - c0:BT - c0], ACT.Copy)
                                if b == 1:
                                    act.activation(at_column(ffn_tail_s, 0, col), src[:, ncol - 2 - c0:ncol - c0], ACT.Copy)
                                    act.activation(up_u[:, m, 2 + BT:2 + BT + GAP], at_column(params, FFN_PREV, col), ACT.Copy)
                            act.activation(dst, src[:, 0:n], ACT.Copy,
                                           scale=params[:, FFN_TAP + 2, bass.ds(col, 1)]).then_inc(ffn.up_read, 1)
                            if m == 1:
                                act.wait_ge(ffn.conv_done, g + 1)
                                act.activation(dst, dst, ACT.Silu).then_inc(ffn.silu, 1)
                                act.wait_ge(ffn.h_done, i + 1)
                                if b == 1 and c == nch - 1:
                                    act.activation(hid_s[:, par, 0:DEC], dst[:, n - DEC:n], ACT.Copy)
                                act.activation(hid_hi[:, par, c0:c0 + n], dst, ACT.Copy).then_inc(ffn.h_hi, 1)
                        if nxt is not None:
                            high_unit(act, nxt(m))

                act.preload_act_table(ACT.Silu)
                if b == 0:
                    act.wait_ge(ffn.up_done, 1)
                    act.activation(up_u[:, :, 0:2], zeros4[:, :, :], ACT.Copy)
                ffn_step(0, 0, 0, lambda m: up_unit(b, m, 1))
                with act.Fori(0, (NF - 2) // 2) as i:
                    for d in range(2):
                        f = i * 2 + (1 + d)
                        ffn_step(f, (1 + d) % 2, i + (1 + d) // 2, lambda m, f=f: up_unit(b, m, f + 1))
                ffn_step(NF - 1, (NF - 1) % 2, (NF - 1) // 2, (lambda m: prep["last", m][0]) if b == 0 else None)
                if b == 1:
                    act.preload_act_table_set("natural_log_exp_and_others")
                    for t in range(nt):
                        m = tile_cols(t)[1]
                        act.wait_ge(ffn.bank_free, 4 + 2 * nt * (NF - 1) + 2 * (t + 1))
                        nf.wait(act, "scaled", t - 1)
                        norm_rstd(nf, t, resid[0:m, t, :])

        @block.tensor
        def _(pe):
            def product(out, pairs, first=True, final=True):
                last = None
                for n, (lh, ll, rh, rl) in enumerate(pairs):
                    end = final and n == len(pairs) - 1
                    pe.matmul(out, lh, rh, start=(first and n == 0), stop=False)
                    pe.matmul(out, ll, rh, start=False, stop=False)
                    last = pe.matmul(out, lh, rl, start=False, stop=end)
                return last

            def down_product(bank, t, f, par, cols):
                c0, m = tile_cols(t)
                wh, wl = w_hi[:, 2 + par, cols], w_lo[:, 2 + par, cols]
                if m == P:
                    return product(ps[:, bank, :], [(hid_hi[:, par, c0:c0 + m], hid_lo[:, par, c0:c0 + m], wh, wl)])
                pe.matmul(ps[:, bank, :], hid_s[:, par, :], wh, start=True, stop=False)
                return pe.matmul(ps[:, bank, :], hid_s[:, par, :], wl, start=False, stop=True)

            def columns(s, bank, c0, w):
                return product(ps[:, bank, 0:w], [
                    (w_hi[:, s, k * P:(k + 1) * P], w_lo[:, s, k * P:(k + 1) * P],
                     xt_hi[:, k, c0:c0 + w], xt_lo[:, k, c0:c0 + w]) for k in range(KT)])

            def norm_turn(norm, t):
                m = tile_cols(t)[1]
                norm.wait(pe, "scaled", t + 1)
                for h in range(2):
                    norm.wait(pe, "lo", 2 * (t - 2) + h + 1)
                    for k in range(4):
                        last = pe.transpose(ps[:, 4 + 2 * (t % 2) + h, k * P:k * P + m],
                                            x_n[0:m, t % 2, (4 * h + k) * P:(4 * h + k + 1) * P], ident[0:m, 0:m])
                    last.then_inc(norm.turned, 1)

            pe.wait_ge(consts_ready, 12)

            for b in range(2):
                mix, ffn, n1, n2, nf = mixes[b], ffns[b], first[b], second[b], final[b]
                nt, nch, ncol = TILES[b], len(CHUNKS[b]), NCOL[b]
                for t in range(early_tiles(b)):
                    if b == 1 and t < 2:
                        pe.wait_ge(ffns[0].bank_free, 4 + 2 * TILES[0] * NF - 2 * (1 - t))
                    norm_turn(n1, t)
                    if b == 0 and t == 1:
                        pe.wait_ge(rows_ready, 16 * 12)
                        for i in range(12):
                            last = pe.transpose(ps[:, 2 + i // 6, (i % 6) * 2 * NF:(i % 6 + 1) * 2 * NF], rows[:, i, :],
                                                ident[0:2 * NF, 0:2 * NF])
                        last.then_inc(rows_turned, 1)
                if b == 1:
                    pe.wait_ge(ffns[0].up_read, 2 * len(CHUNKS[0]) * NF)
                groups = z_groups(b)
                for g, (n, c) in enumerate(groups):
                    c0, w = Z_CHUNKS[b][c]
                    if b == 0 and g == 2:
                        pe.wait_ge(params_ready, 2)
                    if n == GATE:
                        pe.wait_ge(gr_ready, 1)
                        wait(pe, mix.z_read, g - 3)
                        for k in range(KT):
                            pe.matmul(ps[0:2 * RANK, g % 4, 0:w], w_gr[:, k, :], xt_hi[:, k, c0:c0 + w], start=(k == 0), stop=False)
                            last = pe.matmul(ps[0:2 * RANK, g % 4, 0:w], w_gr[:, k, :], xt_lo[:, k, c0:c0 + w],
                                             start=False, stop=(k == KT - 1))
                        last.then_inc(mix.z_done, 1)
                        continue
                    if c == 0:
                        pe.wait_ge(lo_ready[n % SLOTS], unit_index(b, "z", n % SLOTS, n // SLOTS) + 1)
                    wait(pe, mix.z_read, g - 3)
                    if n == 0:
                        n1.wait(pe, "lo", 2 * last_tile_of(b, (c0, w)) + 2)
                    columns(n % SLOTS, g % 4, c0, w).then_inc(mix.z_done, 1)
                    if early_tiles(b) + g < nt:
                        norm_turn(n1, early_tiles(b) + g)

                def gate_product(t):
                    c0, m = tile_cols(t)
                    wait(pe, mix.turned_read, t)
                    pe.matmul(ps[0:m, B_GATE, 0:2 * P], gate_in[:, c0:c0 + m], w_al[:, :], start=True, stop=True).then_inc(mix.pre, 1)

                def gate_sums(t):
                    m = tile_cols(t)[1]
                    pe.wait_ge(mix.lg, t + 1)
                    for q in range(2):
                        last = pe.matmul(ps[:, B_GATE, q * P:q * P + m], lg[0:m, q * P:(q + 1) * P], tri[0:m, 0:m], start=True, stop=True)
                    last.then_inc(mix.cum, 1)

                def scores(t):
                    m = tile_cols(t)[1]
                    pe.wait_ge(mix.qk_exp, t + 1)
                    wait(pe, mix.att_read, t)
                    for h in range(HEADS):
                        last = pe.matmul(ps[0:m, B_ATT, h * P:h * P + m], k_exp[:, h // 2, 0:m], q_exp[:, h // 2, h % 2, 0:m],
                                         start=True, stop=True)
                    last.then_inc(mix.att_done, 1)
                    for q in range(2):
                        last = pe.transpose(ps[0:m, B_GATE, q * P:(q + 1) * P], k_end[:, q, 0:m], ident[:, :])
                    last.then_inc(mix.turned, 1)

                def outputs_1(t):
                    m = tile_cols(t)[1]
                    s = gla_s if t < BT // P else gla_s_smp
                    pe.wait_ge(mix.turned_read, t + 1)
                    pe.wait_ge(mix.att_read, t + 1)
                    wait(pe, mix.state0, t)
                    wait(pe, mix.state1, t)
                    wait(pe, mix.gla_y, t)
                    for h in range(HEADS):
                        pe.matmul(ps[0:m, B_DS, h * HV:(h + 1) * HV],
                                  k_end_t[0:m, h, 0:m // CHUNK, :].rearrange("p c k -> p (c k)"),
                                  v_tok[0:m, t, h * HV:(h + 1) * HV], start=True, stop=True)
                    for h in range(HEADS):
                        pe.matmul(ps[:, B_O, h * P:h * P + m], v_tok[0:m, t, h * HV:(h + 1) * HV], att[0:m, h, 0:m],
                                  start=(h == 0), stop=False, skip_group_check=True)
                    for h in range(HEADS):
                        last = pe.matmul(ps[:, B_O, h * P:h * P + CHUNK], s[:, h // 2, :], q_exp[:, h // 2, h % 2, 0:CHUNK],
                                         start=False, stop=(m == CHUNK), skip_group_check=True)
                    last.then_inc(mix.d1, 1)

                def outputs_2(t):
                    pe.wait_ge(mix.state0, t + 1)
                    for h in range(HEADS):
                        last = pe.matmul(ps[:, B_O, h * P + CHUNK:(h + 1) * P], gla_s[:, h // 2, :],
                                         q_exp[:, h // 2, h % 2, CHUNK:P], start=False, stop=True, skip_group_check=True)
                    last.then_inc(mix.d2, 1)

                def mean_squares(t):
                    m = tile_cols(t)[1]
                    pe.wait_ge(mix.o_squared, t + 1)
                    wait(pe, mix.o_rs, 2 * t)
                    pe.matmul(ps[:, B_MEAN, 0:HEADS * m].rearrange("p (h c) -> p h c", h=HEADS), ones[:, :], o_sq[:, :, 0:m],
                              start=True, stop=True).then_inc(mix.o_mean, 1)

                ng = len(groups)
                for t in range(nt):
                    c0, m = tile_cols(t)
                    pe.wait_ge(mix.z_read, ng + t - 2 if t >= 3 else max(g for g in range(ng) if g % 4 == t) + 1)
                    for i in range(SLOTS):
                        s = (NZ + i) % SLOTS
                        if t == 0:
                            pe.wait_ge(lo_ready[s], unit_index(b, "v", s, 0) + 1)
                        last = product(ps[0:m, t % 3, :], [
                            (xt_hi[:, 2 * s + k, c0:c0 + m], xt_lo[:, 2 * s + k, c0:c0 + m],
                             w_hi[:, s, k * 512:(k + 1) * 512], w_lo[:, s, k * 512:(k + 1) * 512]) for k in range(2)],
                            first=(i == 0), final=(i == SLOTS - 1))
                    last.then_inc(mix.z_done, 1)
                    if t == T_PRODUCT:
                        pe.wait_ge(mix.z_read, ng)
                        if b == 0:
                            pe.wait_ge(small_ready, 64)
                        gate_product(0)
                    if t == T_SUMS:
                        gate_sums(0)
                    if t == T_SCORES:
                        scores(0)
                pe.wait_ge(mix.z_read, ng + nt)
                for j in range(CJ):
                    for ev in conv_events(b, j):
                        if ev[0] == "G":
                            _, m, c = ev
                            c0, w = CHUNKS[b][c]
                            gi = (3 * j + m) * nch + c
                            if c == 0:
                                pe.wait_ge(lo_ready[m], unit_index(b, "conv", m, j) + 1)
                            if gi >= 3:
                                pj, pm, pc = (gi - 3) // (3 * nch), (gi - 3) // nch % 3, (gi - 3) % nch
                                pe.wait_ge((mix.cg_read, mix.u_done, mix.y_done)[pm], pj * nch + pc + 1)
                            columns(m, gi % 3, c0, w).then_inc(mix.c_done, 1)
                            continue
                        t = ev[1]
                        more = t + 1 < nt
                        if ev[0] == "X":
                            outputs_1(t)
                            if more:
                                gate_product(t + 1)
                        if ev[0] == "Y":
                            outputs_2(t)
                            if more:
                                gate_sums(t + 1)
                        if ev[0] == "Z":
                            mean_squares(t)
                            if more:
                                scores(t + 1)
                pe.wait_ge(mix.u_done, CJ * nch)
                pe.wait_ge(mix.y_done, CJ * nch)
                n = 0
                for p in range(4):
                    ks = [(2 * p + i + HEADS) % KT for i in range(2)]
                    ss = [(2 * p + i) % SLOTS for i in range(2)]
                    for i in range(2):
                        pe.wait_ge(lo_ready[ss[i]], unit_index(b, "out", ss[i], (2 * p + i) // SLOTS) + 1)
                    if p:
                        pe.wait_ge(mix.y_lo, 2 * p)
                    for t in range(nt):
                        c0, m = tile_cols(t)
                        if p == 0:
                            pe.wait_ge(mix.y_lo_first, 2 * (chunk_of_end(b, t) + 1))
                        for h in range(2):
                            wait(pe, mix.out_read, n - 3)
                            product(ps[0:m, n % 4, :], [
                                (xt_hi[:, k, c0:c0 + m], xt_lo[:, k, c0:c0 + m],
                                 w_hi[:, s, h * 512:(h + 1) * 512], w_lo[:, s, h * 512:(h + 1) * 512])
                                for k, s in zip(ks, ss)]).then_inc(mix.out_done, 1)
                            n += 1
                        if p == 0 and t % 3 == 2 and t // 3 < nch:
                            c = t // 3
                            pe.wait_ge(mix.csum, 2 * c + 2)
                            pe.matmul(ps[:, 4 + c, 0:CHUNKS[b][c][1]], ones[:, :], conv_sq[:, 0, 0:CHUNKS[b][c][1]],
                                      start=True, stop=True).then_inc(mix.cmean, 1)
                        if p == 3 and t >= 2:
                            norm_turn(n2, t - 2)

                def down(f, par, pair, share):
                    for n in share:
                        t, h = n // 2, n % 2
                        c0, m = tile_cols(t)
                        if n == 0:
                            pe.wait_ge(lo_ready[2 + par], unit_index(b, "ffn", 2 + par, 0) + pair + 1)
                        if h == 0:
                            pe.wait_ge(ffn.h_lo, f * nch + (chunk_of_end(b, t) + 1))
                        bank = 4 + (par * 2 * nt + n) % 4
                        pe.wait_ge(ffn.bank_free, f * (2 * nt) + (n + 1))
                        s = slice(h * 512, (h + 1) * 512)
                        down_product(bank, t, f, par, s).then_inc(ffn.down_done, 1)

                def ffn_step(f, par, pair):
                    first_f = isinstance(f, int) and f == 0
                    for m in range(2):
                        pe.wait_ge(lo_ready[m], unit_index(b, "ffn", m, 0) + f + 1)
                        for c, (c0, n) in enumerate(CHUNKS[b]):
                            slot = m * nch + c
                            g = f * (2 * nch) + slot
                            if first_f and slot < 4:
                                pe.wait_ge(mix.out_read, 8 * nt - 3 + slot)
                            else:
                                pe.wait_ge(ffn.up_read, g - 3)
                            if first_f and m == 0:
                                n2.wait(pe, "lo", 2 * last_tile_of(b, (c0, n)) + 2)
                            columns(m, (par * 2 * nch + slot) % 4, c0, n).then_inc(ffn.up_done, 1)
                            if first_f and slot == 0:
                                norm_turn(n2, nt - 2)
                                norm_turn(n2, nt - 1)
                            if not first_f:
                                down(f - 1, 1 - par, pair + (par - 1), down_share(b, slot))

                ffn_step(0, 0, 0)
                with pe.Fori(0, (NF - 2) // 2) as i:
                    for d in range(2):
                        ffn_step(i * 2 + (1 + d), (1 + d) % 2, i + (1 + d) // 2)
                ffn_step(NF - 1, (NF - 1) % 2, (NF - 1) // 2)
                down(NF - 1, (NF - 1) % 2, (NF - 1) // 2, range(TAILS_AT))
                if b == 1:
                    pe.wait_ge(ffn.up_read, 2 * nch * NF)
                    for i in range(8):
                        src = (ffn_tail, ffn_tail_s, conv_tail, conv_tail_s)[i // 2]
                        w = 2 * NF if i < 4 else CJ
                        last = pe.transpose(ps[0:w, i // 4, (i % 4) * P:(i % 4 + 1) * P], src[:, i % 2, :], ident[:, :])
                        if i % 4 == 3:
                            last.then_inc(tails_turned, 1)
                down(NF - 1, (NF - 1) % 2, (NF - 1) // 2, range(TAILS_AT, 2 * nt))

        @block.vector
        def _(dve):
            def norm_scale(norm, t, src):
                m = tile_cols(t)[1]
                norm.wait(dve, "rstd", t + 1)
                dve.scalar_tensor_tensor(x_n[0:m, t % 2, :], src, rstd[0:m, t % 2:t % 2 + 1], gain[0:m, :],
                                         ALU.mult, ALU.mult).then_inc(norm.scaled, 1)

            def norm_low(norm, t):
                c0, m = tile_cols(t)
                for h in range(2):
                    norm.wait(dve, "hi", 2 * t + h + 1)
                    k = slice(4 * h, 4 * h + 4)
                    dve.tensor_tensor(xt_lo[:, k, c0:c0 + m],
                                      ps[:, 4 + 2 * (t % 2) + h, :].rearrange("p (k c) -> p k c", k=4)[:, :, 0:m],
                                      xt_hi[:, k, c0:c0 + m].bitcast(F32), ALU.subtract).then_inc(norm.lo, 1)

            for b in range(2):
                mix, ffn, n1, n2, nf = mixes[b], ffns[b], first[b], second[b], final[b]
                nt, nch, ncol = TILES[b], len(CHUNKS[b]), NCOL[b]
                if b == 0:
                    dve.wait_ge(gain_ready, 16)
                else:
                    norm_low(n1, 0)
                for t in range(2 * b, nt):
                    m = tile_cols(t)[1]
                    n1.wait(dve, "turned", 2 * (t - 1))
                    norm_scale(n1, t, x_in[0:m, t % NX, :])
                    if t:
                        norm_low(n1, t - 1)
                    if b == 0 and t == 2:
                        dve.wait_ge(rows_turned, 1)
                        for h in range(2):
                            dve.tensor_copy(params[:, 6 * h:6 * h + 6, :].rearrange("p a f -> p (a f)"),
                                            ps[:, 2 + h, 0:12 * NF]).then_inc(params_ready, 1)
                norm_low(n1, nt - 1)
                if b == 1:
                    dve.wait_ge(gain_ready, 16 * 4)
                    n1.wait(dve, "turned", 2 * nt)
                    for t in range(TILES[0]):
                        if t >= 2:
                            dve.wait_ge(stored[t % 2], 16 * (t // 2))
                        norm_scale(final[0], t, resid[:, t, :])
                if b == 0:
                    dve.wait_ge(small_ready, 64)
                    dve.wait_ge(params_ready, 2)
                dve.wait_ge(mix.zeros, 3)

                def pre_gate(t):
                    m = tile_cols(t)[1]
                    dve.wait_ge(mix.pre, t + 1)
                    wait(dve, mix.cum, t)
                    dve.tensor_tensor(lg[0:m, :], ps[0:m, B_GATE, 0:2 * P], b_al[0:m, :], ALU.add).then_inc(mix.pre_b, 1)

                def log_gate(t):
                    m = tile_cols(t)[1]
                    dve.wait_ge(mix.soft, 3 * t + 3)
                    dve.scalar_tensor_tensor(lg[0:m, :], lg[0:m, :], 0.0, soft[0:m, :], ALU.min, ALU.subtract).then_inc(mix.lg, 1)

                def decays(t):
                    c0, m = tile_cols(t)
                    ch = m // CHUNK
                    dve.wait_ge(mix.cum_read, t + 1)
                    bv = b_cum[:, :, 0:m].rearrange("p q (c i) -> p q c i", c=ch)
                    for q in range(2):
                        last = dve.tensor_tensor(k_end[:, q, 0:m].rearrange("p (c i) -> p c i", c=ch), bv[:, q],
                                                 bv[:, q, :, CHUNK - 1:CHUNK].to_broadcast([P, ch, CHUNK]), ALU.subtract)
                    last.then_inc(mix.dist, 1)
                    dve.tensor_tensor(q_exp[0:HK, :, 0, 0:m], q_exp[0:HK, :, 0, 0:m], qk[0:HK, 0:2, c0:c0 + m], ALU.mult)
                    dve.tensor_tensor(q_exp[HK:P, :, 1, 0:m], q_exp[HK:P, :, 1, 0:m], qk[HK:P, 0:2, c0:c0 + m], ALU.mult)
                    dve.tensor_tensor(k_exp[:, :, 0:m], k_exp[:, :, 0:m], qk[:, 2:4, c0:c0 + m], ALU.mult)
                    dve.wait_ge(mix.k_end_exp, t + 1)
                    dve.tensor_tensor(k_end[:, :, 0:m], k_end[:, :, 0:m], qk[:, 2:4, c0:c0 + m], ALU.mult).then_inc(mix.qk_exp, 1)

                def masked_scores(t):
                    m = tile_cols(t)[1]
                    dve.wait_ge(mix.att_done, t + 1)
                    for h in range(HEADS):
                        last = dve.copy_predicated(att[0:m, h, 0:m], tri[0:m, 0:m].bitcast(U32), ps[0:m, B_ATT, h * P:h * P + m])
                    last.then_inc(mix.att_read, 1)

                def next_state(t, c):
                    s = gla_s if t < BT // P else gla_s_smp
                    dve.wait_ge((mix.d1, mix.d2)[c], t + 1)
                    for q in range(2):
                        for e in range(2):
                            r = slice(e * HK, (e + 1) * HK)
                            h = 2 * q + e
                            last = dve.scalar_tensor_tensor(s[r, q, :], s[r, q, :], decay[r, q, c:c + 1],
                                                            ps[c * HK:(c + 1) * HK, B_DS, h * HV:(h + 1) * HV], ALU.mult, ALU.add)
                    last.then_inc((mix.state0, mix.state1)[c], 1)

                def gla_out(t):
                    c0, m = tile_cols(t)
                    dve.wait_ge(mix.o_rs, 2 * t + 2)
                    dve.scalar_tensor_tensor(o_sq[:, :, 0:m], ps[:, B_O, :].rearrange("p (h c) -> p h c", h=HEADS)[:, :, 0:m],
                                             params[:, G_GLA, 0:1], o_sq[:, :, 0:m], ALU.mult, ALU.mult).then_inc(mix.gla_step, 1)
                    dve.wait_ge(mix.gla_step, t + 1)
                    dve.tensor_tensor(gla_y[:, :, c0:c0 + m], gla_y[:, :, c0:c0 + m], o_sq[:, :, 0:m], ALU.mult).then_inc(mix.gla_y, 1)

                def first_lows(c):
                    for n in range(2):
                        dve.wait_ge(mix.y_hi, 2 * c + n + 1)
                        low_part(dve, n, *CHUNKS[b][c]).then_inc(mix.y_lo_first, 1)

                pre_gate(0)
                log_gate(0)
                decays(0)
                masked_scores(0)
                for j in range(CJ):
                    for ev in conv_events(b, j):
                        if ev[0] == "G":
                            _, m, c = ev
                            c0, w = CHUNKS[b][c]
                            gi = (3 * j + m) * nch + c
                            i = j * nch + c
                            y = conv_y[:, j, c0:c0 + w]
                            src = ps[:, gi % 3, 0:w]
                            if m == 1:
                                if c == 0:
                                    dve.tensor_copy(conv_u[:, 0:2], conv_tail[:, :, j])
                                dve.wait_ge(mix.c_done, gi + 1)
                                dve.wait_ge(mix.cg_read, i + 1)
                                dve.tensor_tensor(conv_u[:, 2 + c0:2 + c0 + w], src, y, ALU.mult).then_inc(mix.u_done, 1)
                                dve.wait_ge(mix.u_done, i + 1)
                                if c == nch - 1:
                                    dve.tensor_copy(conv_tail[:, :, j], conv_u[:, BT:BT + 2])
                                    if b == 1:
                                        dve.tensor_copy(conv_tail_s[:, :, j], conv_u[:, ncol:ncol + 2])
                                        dve.tensor_copy(conv_u[:, 2 + BT:2 + BT + GAP],
                                                        params[:, CONV_PREV:CONV_PREV + 2, j]).then_inc(mix.gap, 1)
                                        dve.wait_ge(mix.gap, j + 1)
                                for tap in (2, 1, 0):
                                    wt = params[:, CONV_TAP + tap, j:j + 1]
                                    u = conv_u[:, c0 + tap:c0 + tap + w]
                                    if tap == 2:
                                        last = dve.tensor_scalar(y, u, wt, None, ALU.mult)
                                    else:
                                        last = dve.scalar_tensor_tensor(y, u, wt, y, ALU.mult, ALU.add)
                                    last.then_inc(mix.conv_step, 1)
                                    dve.wait_ge(mix.conv_step, 3 * i + 3 - tap)
                            if m == 2:
                                if j == CJ - 1 and c:
                                    first_lows(c - 1)
                                dve.wait_ge(mix.c_done, gi + 1)
                                dve.tensor_tensor(y, src, y, ALU.mult).then_inc(mix.y_done, 1)
                            continue
                        t = ev[1]
                        more = t + 1 < nt
                        if ev[0] == "X":
                            next_state(t, 0)
                            if more:
                                pre_gate(t + 1)
                                log_gate(t + 1)
                        if ev[0] == "Y":
                            next_state(t, 1)
                            if more:
                                decays(t + 1)
                        if ev[0] == "Z":
                            if more:
                                masked_scores(t + 1)
                            gla_out(t)
                first_lows(nch - 1)
                n_out = 0

                def conv_norm():
                    dve.wait_ge(mix.crs, nch)
                    for j in range(CJ):
                        dve.scalar_tensor_tensor(conv_y[:, j, 0:ncol], conv_y[:, j, 0:ncol], params[:, G_CONV, j:j + 1],
                                                 rs_conv[:, 0:ncol], ALU.mult, ALU.mult).then_inc(mix.cy, 1)

                for p in range(4):
                    for t in range(nt):
                        m = tile_cols(t)[1]
                        if p == 0:
                            dve.wait_ge(mix.x_in[t % 2], 16 * (t // 2 + 1))
                        for h in range(2):
                            s = slice(h * 512, (h + 1) * 512)
                            dve.wait_ge(mix.out_done, n_out + 1)
                            prev = x_in[0:m, 1 + t % 2, s] if p == 0 else resid[0:m, t, s]
                            dve.tensor_tensor(resid[0:m, t, s], ps[0:m, n_out % 4, :], prev, ALU.add).then_inc(mix.out_read, 1)
                            n_out += 1
                        if p == 0 and t % 3 == 1 and t // 3 < nch:
                            c = t // 3
                            w = CHUNKS[b][c][1]
                            dve.wait_ge(mix.csq, c + 1)
                            dve.tensor_tensor(conv_sq[:, 0:2, 0:w], conv_sq[:, 0:2, 0:w], conv_sq[:, 2:4, 0:w],
                                              ALU.add).then_inc(mix.csum, 1)
                            dve.wait_ge(mix.csum, 2 * c + 1)
                            dve.tensor_tensor(conv_sq[:, 0, 0:w], conv_sq[:, 0, 0:w], conv_sq[:, 1, 0:w],
                                              ALU.add).then_inc(mix.csum, 1)
                        if p == 0 and t == nt - 1:
                            conv_norm()
                        if p == 3:
                            if t == 0:
                                dve.wait_ge(gain_ready, 16 * (3 * b + 2))
                            if t >= 1:
                                n2.wait(dve, "turned", 2 * (t - 2))
                                norm_scale(n2, t - 1, resid[0:tile_cols(t - 1)[1], t - 1, :])
                            if t >= 3:
                                norm_low(n2, t - 3)
                n2.wait(dve, "turned", 2 * (nt - 2))
                norm_scale(n2, nt - 1, resid[0:tile_cols(nt - 1)[1], nt - 1, :])
                norm_low(n2, nt - 3)
                norm_low(n2, nt - 2)
                norm_low(n2, nt - 1)

                def add_down(f, par, share):
                    for n in share:
                        t, h = n // 2, n % 2
                        m = tile_cols(t)[1]
                        s = slice(h * 512, (h + 1) * 512)
                        dve.wait_ge(ffn.down_done, f * (2 * nt) + (n + 1))
                        bank = 4 + (par * 2 * nt + n) % 4
                        last = dve.tensor_tensor(resid[0:m, t, s], resid[0:m, t, s], ps[0:m, bank, :], ALU.add)
                        if m == DEC:
                            last.then_inc(ffn.half, 1)
                            dve.wait_ge(ffn.half, f * 2 + (h + 1))
                            last = dve.tensor_tensor(resid[0:m, t, s], resid[0:m, t, s], ps[m:2 * m, bank, :], ALU.add)
                        last.then_inc(ffn.bank_free, 1)

                def ffn_step(f, par):
                    first_f = isinstance(f, int) and f == 0
                    for m in range(2):
                        for c, (c0, n) in enumerate(CHUNKS[b]):
                            slot = m * nch + c
                            g = f * (2 * nch) + slot
                            y = up_a[:, c0:c0 + n] if m == 0 else up_g[:, (par * nch + c) % 2, 0:n]
                            col = m * NF + f
                            dve.wait_ge(ffn.up_read, g + 1)
                            dve.scalar_tensor_tensor(y, up_u[:, m, c0 + 1:c0 + 1 + n], params[:, FFN_TAP + 1, bass.ds(col, 1)], y,
                                                     ALU.mult, ALU.add).then_inc(ffn.tap1, 1)
                            dve.wait_ge(ffn.tap1, g + 1)
                            dve.scalar_tensor_tensor(y, up_u[:, m, c0:c0 + n], params[:, FFN_TAP, bass.ds(col, 1)], y,
                                                     ALU.mult, ALU.add).then_inc(ffn.conv_done, 1)
                            if not first_f:
                                add_down(f - 1, 1 - par, down_share(b, slot))
                            if m == 1:
                                dve.wait_ge(ffn.silu, f * nch + (c + 1))
                                dve.tensor_tensor(y, y, up_a[:, c0:c0 + n], ALU.mult).then_inc(ffn.h_done, 1)

                dve.memset(msq[:, 0:1], 0.0).then_inc(ffn.bank_free, 4)
                ffn_step(0, 0)
                with dve.Fori(0, (NF - 2) // 2) as i:
                    for d in range(2):
                        ffn_step(i * 2 + (1 + d), (1 + d) % 2)
                ffn_step(NF - 1, (NF - 1) % 2)
                if b == 0:
                    for t in range(nt):
                        add_down(NF - 1, (NF - 1) % 2, range(2 * t, 2 * t + 2))
                        if t == nt - 3:
                            dve.wait_ge(gain_ready, 16 * 3)
                            norm_scale(first[1], 0, x_in[:, 0, :])
                    norm_scale(first[1], 1, x_in[:, 1, :])
                else:
                    dve.wait_ge(gain_ready, 16 * 6)
                    for t in range(nt + 1):
                        if 2 * t == TAILS_AT + 2:
                            dve.wait_ge(tails_turned, 2)
                            dve.tensor_copy(tails_out[:, 0:4, :].rearrange("p a c -> p (a c)"), ps[0:2 * NF, 0, :]).then_inc(tails_ready, 1)
                            dve.tensor_copy(tails_out[0:CJ, 4:8, :].rearrange("p a c -> p (a c)"), ps[0:CJ, 1, :]).then_inc(tails_ready, 1)
                        if t < nt:
                            add_down(NF - 1, (NF - 1) % 2, range(2 * t, 2 * t + 2))
                        if t:
                            m = tile_cols(t - 1)[1]
                            dve.wait_ge(stored[(t - 1) % 2], 16 * (TILES[0] // 2 + (t - 1) // 2))
                            norm_scale(nf, t - 1, resid[0:m, t - 1, :])


_INS = ["x_prompt", "x_sample", "state_conv", "state_gla", "state_ffn_conv", "w_in", "w_alpha", "b_alpha", "conv_w",
        "g_conv", "g_gla", "w_out", "norm1", "norm2", "w_up", "ffn_conv_w", "w_down", "final_norm"]
_OUTS = [(1, SEQ, D), (1, DEC, D), (1, 1, 2, D_CONV), (1, 1, HEADS, HK, HV), (1, 1, 2, 2 * D_FF),
         (1, 1, 2, D_CONV), (1, 1, HEADS, HK, HV), (1, 1, 2, 2 * D_FF)]


def kernel(**inputs):
    import numpy as _np
    import concourse.bacc as _bacc
    from concourse.bass_utils import run_bass_kernel_spmd as _run

    nc = _bacc.Bacc("TRN2", target_bir_lowering=False, num_devices=1, dynamic_dma_scratch_size=1024)
    arrays, args = {}, []
    for name in _INS:
        a = _np.ascontiguousarray(inputs[name])
        arrays[f"in_{name}_dram"] = a
        args.append(nc.dram_tensor(f"in_{name}_dram", a.shape, mybir.dt.from_np(a.dtype), kind="ExternalInput").ap())
    for i, shape in enumerate(_OUTS):
        args.append(nc.dram_tensor(f"out_{i}_dram", shape, F32, kind="ExternalOutput").ap())
    build(nc, *args)
    r = _run(nc, [arrays], core_ids=[0])
    return tuple(r.results[0][f"out_{i}_dram"] for i in range(len(_OUTS)))
```
